# Optimizing a Trainium2 kernel written in Bass

```python
import math
import jax, jax.numpy as jnp
from jax import lax
import numpy as np

D_MODEL = 1024
BATCH = 1
SEQ = 256
DEPTH = 2

CHUNK = 64
Q_BLOCK = 128
HEAD_DIM = 64
FOX_HEADS = 8
FOX_DIM = FOX_HEADS * HEAD_DIM
GLA_HEADS = 4
GLA_DK = 64
GLA_DV = 128
GLA_QK = GLA_HEADS * GLA_DK
GLA_V = GLA_HEADS * GLA_DV
GLA_RANK = 16
GLA_TAU = 16.0
MIX_WIDTH = FOX_DIM + GLA_V
IN_COLS = 3 * FOX_DIM + FOX_HEADS + 2 * GLA_QK + 2 * GLA_V + GLA_RANK
S5_GROUP = 16
S5_GROUPS = D_MODEL // S5_GROUP
S5_STATE = 64
D_FF = 2816
N_EXPERTS = 8
TOP_K = 2
EXPERT_FF = 2816
N_EVEN = (DEPTH + 1) // 2
N_ODD = DEPTH // 2
EPS = 1e-6


def rmsnorm(x, w):
    xf = x.astype(jnp.float32)
    y = xf * lax.rsqrt(jnp.mean(xf * xf, axis=-1, keepdims=True) + EPS)
    return y * w.astype(jnp.float32)

def adaln(c, w, b):
    m = jax.nn.silu(c.astype(jnp.float32)) @ w + b
    shift, scale, gate = jnp.split(m, 3, axis=-1)
    return shift[:, None, :], scale[:, None, :], gate[:, None, :]

def fox_attention(q, k, v, logf):
    B, H, S, dh = q.shape
    cum = jnp.cumsum(logf, axis=-1)
    nb = S // Q_BLOCK
    qb = q.reshape(B, H, nb, Q_BLOCK, dh).transpose(2, 0, 1, 3, 4)
    cb = cum.reshape(B, H, nb, Q_BLOCK).transpose(2, 0, 1, 3)
    kpos = jnp.arange(S)
    scale = dh ** -0.5

    def block(args):
        i, qi, ci = args
        s = jnp.einsum('bhqd,bhkd->bhqk', qi, k) * scale + ci[..., None] - cum[:, :, None, :]
        qpos = i * Q_BLOCK + jnp.arange(Q_BLOCK)
        s = jnp.where(kpos[None, :] <= qpos[:, None], s, -jnp.inf)
        p = jax.nn.softmax(s, axis=-1)
        return jnp.einsum('bhqk,bhkd->bhqd', p, v)

    out = lax.map(block, (jnp.arange(nb), qb, cb))
    return out.transpose(1, 2, 0, 3, 4).reshape(B, H, S, dh)

def gla_attention(q, k, v, log_a):
    B, H, S, dk = q.shape
    dv = v.shape[-1]
    nc = S // CHUNK

    def to_chunks(t):
        return t.reshape(B, H, nc, CHUNK, t.shape[-1]).transpose(2, 0, 1, 3, 4)

    qc, kc, vc, ac = (to_chunks(q * dk ** -0.5), to_chunks(k), to_chunks(v), to_chunks(log_a))
    bc = jnp.cumsum(ac, axis=3)
    causal = jnp.tril(jnp.ones((CHUNK, CHUNK), dtype=bool))

    def step(state, inp):
        qi, ki, vi, bi = inp
        diff = bi[:, :, :, None, :] - bi[:, :, None, :, :]
        decay = jnp.exp(jnp.where(causal[None, None, :, :, None], diff, -jnp.inf))
        attn = jnp.einsum('bhtd,bhsd,bhtsd->bhts', qi, ki, decay)
        o = (jnp.einsum('bhts,bhsv->bhtv', attn, vi)
             + jnp.einsum('bhtd,bhdv->bhtv', qi * jnp.exp(bi), state))
        blast = bi[:, :, -1:, :]
        state = (jnp.exp(blast[:, :, 0, :])[..., None] * state
                 + jnp.einsum('bhsd,bhsv->bhdv', ki * jnp.exp(blast - bi), vi))
        return state, o

    s0 = jnp.zeros((B, H, dk, dv), jnp.float32)
    _, o = lax.scan(step, s0, (qc, kc, vc, bc))
    return o.transpose(1, 2, 0, 3, 4).reshape(B, H, S, dv)

def even_mixer(h, w_in, fox_fb, gla_w2, gla_b2, gla_norm, w_o):
    B, S, _ = h.shape
    sizes = (FOX_DIM, FOX_DIM, FOX_DIM, FOX_HEADS, GLA_QK, GLA_QK, GLA_V, GLA_V, GLA_RANK)
    cuts = [sum(sizes[:i + 1]) for i in range(len(sizes) - 1)]
    fq, fk, fv, ff, gq, gk, gv, gg, glr = jnp.split(h @ w_in, cuts, axis=-1)

    def heads(t, n):
        return t.reshape(B, S, n, -1).transpose(0, 2, 1, 3)

    logf = jax.nn.log_sigmoid(ff + fox_fb).transpose(0, 2, 1)
    fox = fox_attention(heads(fq, FOX_HEADS), heads(fk, FOX_HEADS), heads(fv, FOX_HEADS), logf)
    fox = fox.transpose(0, 2, 1, 3).reshape(B, S, FOX_DIM)
    log_a = jax.nn.log_sigmoid(glr @ gla_w2 + gla_b2) / GLA_TAU
    gla = gla_attention(heads(gq, GLA_HEADS), heads(gk, GLA_HEADS), heads(gv, GLA_HEADS),
                        heads(log_a, GLA_HEADS))
    gla = rmsnorm(gla.transpose(0, 2, 1, 3), gla_norm).reshape(B, S, GLA_V) * jax.nn.silu(gg)
    return jnp.concatenate([fox, gla], axis=-1) @ w_o

def s5_mixer(h, w_in, lam_re, lam_im, log_dt, b_re, b_im, c_re, c_im, d_skip, w_glu, w_o):
    B, S, _ = h.shape
    f32 = jnp.float32
    lam_re, lam_im, log_dt = lam_re.astype(f32), lam_im.astype(f32), log_dt.astype(f32)
    b_re, b_im, c_re, c_im = b_re.astype(f32), b_im.astype(f32), c_re.astype(f32), c_im.astype(f32)
    u = h @ w_in
    ug = u.reshape(B, S, S5_GROUPS, S5_GROUP)
    dt = jnp.exp(log_dt)[:, None]
    mag = jnp.exp(lam_re * dt)
    a_re = mag * jnp.cos(lam_im * dt)
    a_im = mag * jnp.sin(lam_im * dt)
    den = lam_re * lam_re + lam_im * lam_im
    nr, ni = a_re - 1.0, a_im
    f_re = (nr * lam_re + ni * lam_im) / den
    f_im = (ni * lam_re - nr * lam_im) / den
    bb_re = f_re[..., None] * b_re - f_im[..., None] * b_im
    bb_im = f_re[..., None] * b_im + f_im[..., None] * b_re
    ut = ug.transpose(1, 0, 2, 3)
    bu_re = jnp.einsum('sbgk,gpk->sbgp', ut, bb_re)
    bu_im = jnp.einsum('sbgk,gpk->sbgp', ut, bb_im)
    ar_t = jnp.broadcast_to(a_re[None, None], (S, 1, S5_GROUPS, S5_STATE))
    ai_t = jnp.broadcast_to(a_im[None, None], (S, 1, S5_GROUPS, S5_STATE))

    def combine(e1, e2):
        a1r, a1i, b1r, b1i = e1
        a2r, a2i, b2r, b2i = e2
        return (a1r * a2r - a1i * a2i,
                a1r * a2i + a1i * a2r,
                a2r * b1r - a2i * b1i + b2r,
                a2r * b1i + a2i * b1r + b2i)

    _, _, xr, xi = lax.associative_scan(combine, (ar_t, ai_t, bu_re, bu_im), axis=0)
    y = jnp.einsum('sbgp,gkp->bsgk', xr, c_re) - jnp.einsum('sbgp,gkp->bsgk', xi, c_im)
    y = y.reshape(B, S, D_MODEL) + d_skip * u
    y = jax.nn.gelu(y)
    y = y * jax.nn.sigmoid(y @ w_glu)
    return y @ w_o

def swiglu(h, w_gate, w_up, w_down):
    return (jax.nn.silu(h @ w_gate) * (h @ w_up)) @ w_down

def moe_swiglu(h, w_router, w_gate, w_up, w_down):
    logits = (h @ w_router).astype(jnp.float32)
    top_val, top_idx = lax.top_k(logits, TOP_K)
    weights = jax.nn.softmax(top_val, axis=-1)
    gates = jnp.sum(jax.nn.one_hot(top_idx, N_EXPERTS, dtype=jnp.float32) * weights[..., None], axis=-2)
    out = jnp.zeros_like(h)
    for e in range(N_EXPERTS):
        out = out + gates[..., e:e + 1] * swiglu(h, w_gate[e], w_up[e], w_down[e])
    return out

def first_inputs(seed: int = 0) -> dict:
    key = jax.random.key(seed)
    ks = iter(jax.random.split(key, 64))
    f32 = jnp.float32

    def nrm(shape, scale):
        return jax.random.normal(next(ks), shape, f32) * scale

    def gain(shape):
        return 1.0 + 0.05 * jax.random.normal(next(ks), shape, f32)

    D = D_MODEL
    NE, NO = N_EVEN, N_ODD
    G, P, K = S5_GROUPS, S5_STATE, S5_GROUP
    mod_s = 0.5 * D ** -0.5
    inp = {}
    inp['x'] = nrm((BATCH, SEQ, D), 1.0)
    inp['c'] = nrm((BATCH, D), 1.0)
    inp['e_norm_mix'] = gain((NE, D))
    inp['e_mod_mix_w'] = nrm((NE, D, 3 * D), mod_s)
    inp['e_mod_mix_b'] = nrm((NE, 3 * D), 0.02)
    inp['e_w_in'] = nrm((NE, D, IN_COLS), D ** -0.5)
    inp['e_fox_fb'] = 2.0 + nrm((NE, FOX_HEADS), 0.5)
    inp['e_gla_w2'] = nrm((NE, GLA_RANK, GLA_QK), GLA_RANK ** -0.5)
    inp['e_gla_b2'] = nrm((NE, GLA_QK), 0.02)
    inp['e_gla_norm'] = gain((NE, GLA_DV))
    inp['e_w_o'] = nrm((NE, MIX_WIDTH, D), MIX_WIDTH ** -0.5)
    inp['e_norm_ffn'] = gain((NE, D))
    inp['e_mod_ffn_w'] = nrm((NE, D, 3 * D), mod_s)
    inp['e_mod_ffn_b'] = nrm((NE, 3 * D), 0.02)
    inp['e_ffn_gate'] = nrm((NE, D, D_FF), D ** -0.5)
    inp['e_ffn_up'] = nrm((NE, D, D_FF), D ** -0.5)
    inp['e_ffn_down'] = nrm((NE, D_FF, D), D_FF ** -0.5)
    inp['o_norm_mix'] = gain((NO, D))
    inp['o_mod_mix_w'] = nrm((NO, D, 3 * D), mod_s)
    inp['o_mod_mix_b'] = nrm((NO, 3 * D), 0.02)
    inp['o_w_in'] = nrm((NO, D, D), D ** -0.5)
    inp['o_lam_re'] = -0.5 + nrm((NO, G, P), 0.01)
    inp['o_lam_im'] = math.pi * jnp.arange(P, dtype=f32)[None, None, :] + nrm((NO, G, P), 0.01)
    inp['o_log_dt'] = jax.random.uniform(next(ks), (NO, G), f32, math.log(1e-3), math.log(1e-1))
    inp['o_b_re'] = nrm((NO, G, P, K), (2.0 * K) ** -0.5)
    inp['o_b_im'] = nrm((NO, G, P, K), (2.0 * K) ** -0.5)
    inp['o_c_re'] = nrm((NO, G, K, P), (2.0 / P) ** 0.5)
    inp['o_c_im'] = nrm((NO, G, K, P), (2.0 / P) ** 0.5)
    inp['o_d_skip'] = nrm((NO, D), 1.0)
    inp['o_w_glu'] = nrm((NO, D, D), D ** -0.5)
    inp['o_w_o'] = nrm((NO, D, D), D ** -0.5)
    inp['o_norm_ffn'] = gain((NO, D))
    inp['o_mod_ffn_w'] = nrm((NO, D, 3 * D), mod_s)
    inp['o_mod_ffn_b'] = nrm((NO, 3 * D), 0.02)
    inp['o_router'] = nrm((NO, D, N_EXPERTS), D ** -0.5)
    inp['o_exp_gate'] = nrm((NO, N_EXPERTS, D, EXPERT_FF), D ** -0.5)
    inp['o_exp_up'] = nrm((NO, N_EXPERTS, D, EXPERT_FF), D ** -0.5)
    inp['o_exp_down'] = nrm((NO, N_EXPERTS, EXPERT_FF, D), EXPERT_FF ** -0.5)
    inp['final_norm'] = gain((D,))
    return inp

def first_block(x, c,
              e_norm_mix, e_mod_mix_w, e_mod_mix_b, e_w_in, e_fox_fb, e_gla_w2, e_gla_b2,
              e_gla_norm, e_w_o, e_norm_ffn, e_mod_ffn_w, e_mod_ffn_b, e_ffn_gate, e_ffn_up,
              e_ffn_down,
              o_norm_mix, o_mod_mix_w, o_mod_mix_b, o_w_in, o_lam_re, o_lam_im, o_log_dt,
              o_b_re, o_b_im, o_c_re, o_c_im, o_d_skip, o_w_glu, o_w_o, o_norm_ffn,
              o_mod_ffn_w, o_mod_ffn_b, o_router, o_exp_gate, o_exp_up, o_exp_down,
              final_norm):
    for i in range(DEPTH):
        j = i // 2
        if i % 2 == 0:
            sh, sc, g = adaln(c, e_mod_mix_w[j], e_mod_mix_b[j])
            h = rmsnorm(x, e_norm_mix[j]) * (1.0 + sc) + sh
            y = even_mixer(h, e_w_in[j], e_fox_fb[j], e_gla_w2[j], e_gla_b2[j], e_gla_norm[j], e_w_o[j])
            x = x + (g * y).astype(x.dtype)
            sh, sc, g = adaln(c, e_mod_ffn_w[j], e_mod_ffn_b[j])
            h = rmsnorm(x, e_norm_ffn[j]) * (1.0 + sc) + sh
            y = swiglu(h, e_ffn_gate[j], e_ffn_up[j], e_ffn_down[j])
            x = x + (g * y).astype(x.dtype)
        else:
            sh, sc, g = adaln(c, o_mod_mix_w[j], o_mod_mix_b[j])
            h = rmsnorm(x, o_norm_mix[j]) * (1.0 + sc) + sh
            y = s5_mixer(h, o_w_in[j], o_lam_re[j], o_lam_im[j], o_log_dt[j], o_b_re[j], o_b_im[j],
                         o_c_re[j], o_c_im[j], o_d_skip[j], o_w_glu[j], o_w_o[j])
            x = x + (g * y).astype(x.dtype)
            sh, sc, g = adaln(c, o_mod_ffn_w[j], o_mod_ffn_b[j])
            h = rmsnorm(x, o_norm_ffn[j]) * (1.0 + sc) + sh
            y = moe_swiglu(h, o_router[j], o_exp_gate[j], o_exp_up[j], o_exp_down[j])
            x = x + (g * y).astype(x.dtype)
    return rmsnorm(x, final_norm).astype(x.dtype)


N_MIXERS = 2
D_PLE = 256
RMS_EPS = 1e-6

SSD_EXPAND = 2
SSD_D_INNER = SSD_EXPAND * D_MODEL
SSD_HEAD_DIM = 64
SSD_HEADS = SSD_D_INNER // SSD_HEAD_DIM
SSD_GROUPS = 8
SSD_D_STATE = 128
SSD_CONV = 5
SSD_CHUNK = 128
SSD_BC = SSD_GROUPS * SSD_D_STATE
SSD_CONV_DIM = SSD_D_INNER + 4 * SSD_BC
SSD_IN_DIM = SSD_D_INNER + SSD_CONV_DIM + 2 * SSD_HEADS

GRID_W = 64
NA_HEAD_DIM = 64
NA_HEADS = D_MODEL // NA_HEAD_DIM
NA_WIN_ROWS = 8
NA_WIN_COLS = 16
NA_QBLOCK_COLS = 16
NA_KBLOCK_COLS = NA_QBLOCK_COLS + NA_WIN_COLS
NA_RPB_ROWS = 2 * NA_WIN_ROWS - 1
NA_RPB_COLS = 2 * NA_WIN_COLS - 1

N_SSD_LAYERS = (DEPTH + 1) // 2
N_NA_LAYERS = DEPTH // 2


def rmsnorm_2(x, g):
    xf = x.astype(jnp.float32)
    y = xf * lax.rsqrt(jnp.mean(xf * xf, axis=-1, keepdims=True) + RMS_EPS)
    return (y * g.astype(jnp.float32)).astype(x.dtype)

def swiglu_2(x, w_gu, w_down):
    g, u = jnp.split(x @ w_gu, 2, axis=-1)
    return (jax.nn.silu(g) * u) @ w_down

def centred_depthwise_conv(x, w, b):
    k, c = w.shape
    y = lax.conv_general_dilated(x, w[:, None, :].astype(x.dtype), window_strides=(1,),
                                 padding=((k // 2, k // 2),),
                                 dimension_numbers=('NWC', 'WIO', 'NWC'),
                                 feature_group_count=c)
    return y + b

def ssd_scan(x, dt, a, b_mat, c_mat):
    bsz, seqlen, nh, hp = x.shape
    ng, ns = b_mat.shape[-2:]
    hg = nh // ng
    q = SSD_CHUNK
    nc = seqlen // q
    xc = x.reshape(bsz, nc, q, ng, hg, hp)
    bc = b_mat.reshape(bsz, nc, q, ng, ns)
    cc = c_mat.reshape(bsz, nc, q, ng, ns)
    dtc = dt.astype(jnp.float32).reshape(bsz, nc, q, ng, hg)
    cum = jnp.cumsum(dtc * a.astype(jnp.float32).reshape(ng, hg), axis=2)
    xdt = xc * dtc[..., None].astype(x.dtype)
    lower = jnp.tril(jnp.ones((q, q), dtype=bool))[:, :, None, None]
    seg = cum[:, :, :, None] - cum[:, :, None, :]
    cb = jnp.einsum('bcqgn,bckgn->bcqkg', cc, bc)
    scores = (cb[..., None] * jnp.exp(jnp.where(lower, seg, -jnp.inf))).astype(x.dtype)
    y_diag = jnp.einsum('bcqkgj,bckgjp->bcqgjp', scores, xdt)
    decay_to_end = jnp.exp(cum[:, :, -1:] - cum)
    states = jnp.einsum('bckgn,bckgjp->bcgjpn', bc, xdt * decay_to_end[..., None].astype(x.dtype))
    chunk_decay = jnp.exp(cum[:, :, -1]).astype(x.dtype)

    def step(carry, inp):
        st, dec = inp
        return carry * dec[..., None, None] + st, carry

    _, prev = lax.scan(step, jnp.zeros_like(states[:, 0]),
                       (jnp.moveaxis(states, 1, 0), jnp.moveaxis(chunk_decay, 1, 0)))
    prev = jnp.moveaxis(prev, 0, 1)
    y_off = jnp.einsum('bcqgn,bcgjpn->bcqgjp', cc, prev) * jnp.exp(cum)[..., None].astype(x.dtype)
    return (y_diag + y_off).reshape(bsz, seqlen, nh, hp)

def ssd_mixer(h, w_in, conv_w, conv_b, dt_bias, a_log, d_skip, norm_g, w_out):
    bsz, seqlen, _ = h.shape
    proj = h @ w_in
    z, xbc, dt_raw = jnp.split(proj, [SSD_D_INNER, SSD_D_INNER + SSD_CONV_DIM], axis=-1)
    xbc = jax.nn.silu(centred_depthwise_conv(xbc, conv_w, conv_b))
    xs, b_f, c_f, b_b, c_b = jnp.split(
        xbc, [SSD_D_INNER, SSD_D_INNER + SSD_BC, SSD_D_INNER + 2 * SSD_BC, SSD_D_INNER + 3 * SSD_BC], axis=-1)
    xs = xs.reshape(bsz, seqlen, SSD_HEADS, SSD_HEAD_DIM)
    grp = lambda t: t.reshape(bsz, seqlen, SSD_GROUPS, SSD_D_STATE)
    flip = lambda t: jnp.flip(t, axis=1)
    dt = jax.nn.softplus(dt_raw.reshape(bsz, seqlen, 2, SSD_HEADS) + dt_bias)
    a = -jnp.exp(a_log.astype(jnp.float32))
    y_fwd = ssd_scan(xs, dt[:, :, 0], a[0], grp(b_f), grp(c_f))
    y_bwd = flip(ssd_scan(flip(xs), flip(dt[:, :, 1]), a[1], flip(grp(b_b)), flip(grp(c_b))))
    y = (y_fwd + y_bwd + xs * d_skip[:, None]).reshape(bsz, seqlen, SSD_D_INNER)
    y = rmsnorm_2(y * jax.nn.silu(z), norm_g)
    return y @ w_out

def neighbourhood_attention(h, w_qkv, q_norm, k_norm, rpb, w_out):
    bsz, seqlen, _ = h.shape
    rows = seqlen // GRID_W
    win_r = min(NA_WIN_ROWS, rows)
    n_cb = GRID_W // NA_QBLOCK_COLS
    qkv = (h @ w_qkv).reshape(bsz, rows, GRID_W, 3, NA_HEADS, NA_HEAD_DIM)
    q = rmsnorm_2(qkv[:, :, :, 0], q_norm) * (NA_HEAD_DIM ** -0.5)
    k = rmsnorm_2(qkv[:, :, :, 1], k_norm)
    v = qkv[:, :, :, 2]
    q_col = np.arange(GRID_W).reshape(n_cb, NA_QBLOCK_COLS)
    win_c0 = np.clip(q_col - NA_WIN_COLS // 2, 0, GRID_W - NA_WIN_COLS)
    kblk_c0 = np.clip(q_col[:, 0] - NA_WIN_COLS // 2, 0, GRID_W - NA_KBLOCK_COLS)
    k_col = kblk_c0[:, None] + np.arange(NA_KBLOCK_COLS)
    kc_b = k_col[:, None, :]
    col_valid = jnp.asarray((kc_b >= win_c0[..., None]) & (kc_b < win_c0[..., None] + NA_WIN_COLS))
    col_rel = jnp.asarray(np.clip(kc_b - q_col[..., None] + NA_WIN_COLS - 1, 0, NA_RPB_COLS - 1))

    def row_block(args):
        r, q_row = args
        r0 = jnp.clip(r - win_r // 2, 0, rows - win_r)
        k_blk = lax.dynamic_slice_in_dim(k, r0, win_r, axis=1)[:, :, k_col]
        v_blk = lax.dynamic_slice_in_dim(v, r0, win_r, axis=1)[:, :, k_col]
        q_blk = q_row.reshape(bsz, n_cb, NA_QBLOCK_COLS, NA_HEADS, NA_HEAD_DIM)
        s = jnp.einsum('bxqhd,brxkhd->bhxqrk', q_blk, k_blk).astype(jnp.float32)
        row_rel = r0 - r + jnp.arange(win_r) + NA_WIN_ROWS - 1
        bias = jnp.transpose(rpb[:, row_rel][:, :, col_rel], (0, 2, 3, 1, 4))
        bias = jnp.where(col_valid[:, :, None, :], bias.astype(jnp.float32), -jnp.inf)
        s = s + bias
        pr = jax.nn.softmax(s.reshape(s.shape[:4] + (-1,)), axis=-1).reshape(s.shape).astype(v.dtype)
        o = jnp.einsum('bhxqrk,brxkhd->bxqhd', pr, v_blk)
        return o.reshape(bsz, GRID_W, NA_HEADS * NA_HEAD_DIM)

    out = lax.map(row_block, (jnp.arange(rows), jnp.moveaxis(q, 1, 0)))
    out = jnp.moveaxis(out, 0, 1).reshape(bsz, seqlen, NA_HEADS * NA_HEAD_DIM)
    return out @ w_out

def second_inputs(seed: int = 0) -> dict:
    key = jax.random.key(seed)
    keys = list(jax.random.split(key, 32))
    nxt = lambda: keys.pop()
    nrm = lambda shape, scale: jax.random.normal(nxt(), shape, jnp.float32) * scale
    gain = lambda shape: 1.0 + nrm(shape, 0.02)
    ns, nn_ = N_SSD_LAYERS, N_NA_LAYERS
    dt0 = jnp.exp(jax.random.uniform(nxt(), (ns, 2, SSD_HEADS), jnp.float32,
                                     minval=math.log(1e-3), maxval=math.log(1e-1)))
    dt_bias = dt0 + jnp.log(-jnp.expm1(-dt0))
    a_log = jnp.log(jax.random.uniform(nxt(), (ns, 2, SSD_HEADS), jnp.float32, minval=1.0, maxval=16.0))
    return {
        "x": nrm((BATCH, SEQ, D_MODEL), 1.0),
        "p": nrm((DEPTH, BATCH, SEQ, D_PLE), 1.0),
        "ffn1_norm": gain((DEPTH, D_MODEL)),
        "ffn1_w_gu": nrm((DEPTH, D_MODEL, 2 * D_FF), D_MODEL ** -0.5),
        "ffn1_w_down": nrm((DEPTH, D_FF, D_MODEL), D_FF ** -0.5),
        "mix_norm": gain((DEPTH, D_MODEL)),
        "ffn2_norm": gain((DEPTH, D_MODEL)),
        "ffn2_w_gu": nrm((DEPTH, D_MODEL, 2 * D_FF), D_MODEL ** -0.5),
        "ffn2_w_down": nrm((DEPTH, D_FF, D_MODEL), D_FF ** -0.5),
        "ple_norm": gain((DEPTH, D_MODEL)),
        "ple_w_gate": nrm((DEPTH, D_MODEL, D_MODEL), D_MODEL ** -0.5),
        "ple_w_proj": nrm((DEPTH, D_PLE, D_MODEL), D_PLE ** -0.5),
        "ple_post_norm": gain((DEPTH, D_MODEL)),
        "ssd_w_in": nrm((ns, D_MODEL, SSD_IN_DIM), D_MODEL ** -0.5),
        "ssd_conv_w": nrm((ns, SSD_CONV, SSD_CONV_DIM), SSD_CONV ** -0.5),
        "ssd_conv_b": nrm((ns, SSD_CONV_DIM), 0.02),
        "ssd_dt_bias": dt_bias,
        "ssd_a_log": a_log,
        "ssd_d": gain((ns, SSD_HEADS)),
        "ssd_norm": gain((ns, SSD_D_INNER)),
        "ssd_w_out": nrm((ns, SSD_D_INNER, D_MODEL), SSD_D_INNER ** -0.5),
        "na_w_qkv": nrm((nn_, D_MODEL, 3 * NA_HEADS * NA_HEAD_DIM), D_MODEL ** -0.5),
        "na_q_norm": gain((nn_, NA_HEAD_DIM)),
        "na_k_norm": gain((nn_, NA_HEAD_DIM)),
        "na_rpb": nrm((nn_, NA_HEADS, NA_RPB_ROWS, NA_RPB_COLS), 0.02),
        "na_w_out": nrm((nn_, NA_HEADS * NA_HEAD_DIM, D_MODEL), (NA_HEADS * NA_HEAD_DIM) ** -0.5),
    }

def second_block(x, p, ffn1_norm, ffn1_w_gu, ffn1_w_down, mix_norm, ffn2_norm, ffn2_w_gu, ffn2_w_down,
              ple_norm, ple_w_gate, ple_w_proj, ple_post_norm,
              ssd_w_in, ssd_conv_w, ssd_conv_b, ssd_dt_bias, ssd_a_log, ssd_d, ssd_norm, ssd_w_out,
              na_w_qkv, na_q_norm, na_k_norm, na_rpb, na_w_out):
    h = x
    for i in range(DEPTH):
        h = h + 0.5 * swiglu_2(rmsnorm_2(h, ffn1_norm[i]), ffn1_w_gu[i], ffn1_w_down[i])
        hn = rmsnorm_2(h, mix_norm[i])
        j = i // N_MIXERS
        if i % N_MIXERS == 0:
            h = h + ssd_mixer(hn, ssd_w_in[j], ssd_conv_w[j], ssd_conv_b[j], ssd_dt_bias[j],
                              ssd_a_log[j], ssd_d[j], ssd_norm[j], ssd_w_out[j])
        else:
            h = h + neighbourhood_attention(hn, na_w_qkv[j], na_q_norm[j], na_k_norm[j],
                                            na_rpb[j], na_w_out[j])
        h = h + 0.5 * swiglu_2(rmsnorm_2(h, ffn2_norm[i]), ffn2_w_gu[i], ffn2_w_down[i])
        gate = jax.nn.sigmoid(rmsnorm_2(h, ple_norm[i]) @ ple_w_gate[i])
        h = h + gate * rmsnorm_2(p[i] @ ple_w_proj[i], ple_post_norm[i])
    return h


def setup_inputs(seed=0):
    out = dict(first_inputs(seed))
    for name, value in second_inputs(seed + 1).items():
        if name != "x":
            out[name + "_2"] = value
    return out


def reference(
    x, c, e_norm_mix, e_mod_mix_w, e_mod_mix_b, e_w_in, e_fox_fb, e_gla_w2, e_gla_b2,
    e_gla_norm, e_w_o, e_norm_ffn, e_mod_ffn_w, e_mod_ffn_b, e_ffn_gate, e_ffn_up, e_ffn_down,
    o_norm_mix, o_mod_mix_w, o_mod_mix_b, o_w_in, o_lam_re, o_lam_im, o_log_dt, o_b_re, o_b_im,
    o_c_re, o_c_im, o_d_skip, o_w_glu, o_w_o, o_norm_ffn, o_mod_ffn_w, o_mod_ffn_b, o_router,
    o_exp_gate, o_exp_up, o_exp_down, final_norm, p_2, ffn1_norm_2, ffn1_w_gu_2, ffn1_w_down_2,
    mix_norm_2, ffn2_norm_2, ffn2_w_gu_2, ffn2_w_down_2, ple_norm_2, ple_w_gate_2, ple_w_proj_2,
    ple_post_norm_2, ssd_w_in_2, ssd_conv_w_2, ssd_conv_b_2, ssd_dt_bias_2, ssd_a_log_2,
    ssd_d_2, ssd_norm_2, ssd_w_out_2, na_w_qkv_2, na_q_norm_2, na_k_norm_2, na_rpb_2,
    na_w_out_2,
):
    x = first_block(
        x, c, e_norm_mix, e_mod_mix_w, e_mod_mix_b, e_w_in, e_fox_fb, e_gla_w2, e_gla_b2,
        e_gla_norm, e_w_o, e_norm_ffn, e_mod_ffn_w, e_mod_ffn_b, e_ffn_gate, e_ffn_up,
        e_ffn_down, o_norm_mix, o_mod_mix_w, o_mod_mix_b, o_w_in, o_lam_re, o_lam_im, o_log_dt,
        o_b_re, o_b_im, o_c_re, o_c_im, o_d_skip, o_w_glu, o_w_o, o_norm_ffn, o_mod_ffn_w,
        o_mod_ffn_b, o_router, o_exp_gate, o_exp_up, o_exp_down, final_norm,
    )
    return second_block(
        x, p_2, ffn1_norm_2, ffn1_w_gu_2, ffn1_w_down_2, mix_norm_2, ffn2_norm_2, ffn2_w_gu_2,
        ffn2_w_down_2, ple_norm_2, ple_w_gate_2, ple_w_proj_2, ple_post_norm_2, ssd_w_in_2,
        ssd_conv_w_2, ssd_conv_b_2, ssd_dt_bias_2, ssd_a_log_2, ssd_d_2, ssd_norm_2,
        ssd_w_out_2, na_w_qkv_2, na_q_norm_2, na_k_norm_2, na_rpb_2, na_w_out_2,
    )


_drawn_inputs = setup_inputs


def setup_inputs(seed=0):
    import zlib

    import numpy as np

    out = dict(_drawn_inputs(seed))
    spreads = {}
    factors = {'e_gla_b2': 8.0,
     'e_gla_norm': 3.807,
     'o_norm_mix': 6.099,
     'o_mod_mix_b': 3.305,
     'o_lam_re': 64.0,
     'o_log_dt': 2.887,
     'o_b_re': 3.283,
     'o_c_re': 2.778,
     'o_c_im': 3.23,
     'ffn1_norm_2': 4.876,
     'mix_norm_2': 2.843,
     'ffn2_norm_2': 7.508,
     'ple_norm_2': 58.613,
     'ple_post_norm_2': 44.857,
     'ssd_d_2': 64.0,
     'ssd_norm_2': 3.977,
     'na_q_norm_2': 28.363,
     'na_k_norm_2': 28.62,
     'na_rpb_2': 64.0,
     'ssd_conv_b_2': 5.815}
    for name, (base, spread) in spreads.items():
        noise = np.random.default_rng([zlib.crc32(name.encode()), seed]).standard_normal(out[name].shape)
        drawn = base * np.exp(spread * noise) if base else spread * noise
        out[name] = __import__('jax').numpy.asarray(drawn.astype(out[name].dtype))
    for name, factor in factors.items():
        out[name] = (out[name] * factor).astype(out[name].dtype)
    return out
```

```python
import math
from contextlib import ExitStack

import concourse.bass as bass
from concourse import mybir

F32 = mybir.dt.float32
F32R = mybir.dt.float32r
I32 = mybir.dt.int32
U32 = mybir.dt.uint32
ALU = mybir.AluOpType
ACT = mybir.ActivationFunctionType

P = 128
D = 1024
T = 256
FF = 2816
KD = D // P
KF = FF // P
COLS = 256
SETS = 3
GU_UNITS = FF // COLS
DN_UNITS = D // COLS
E_EXP = 8
EPS = 1e-6
NEG = -1e30

STAGE_UNITS = dict(
    mod_em=6, even_in=7, mod_ef=6, s5_prep=0, even_out=2, even_ffn=15 + 12, s5_tab=0, s5_in=2, s5_glu=2, s5_out=2,
    moe=15 * E_EXP, final=0, ffn1_0=15, ssd_in=17, ssd_out=4, ffn2_0=15, ple_0=4, ffn1_1=15, na_in=6, na_out=2,
    ffn2_1=15, ple_1=4)
ORDER = list(STAGE_UNITS)


class Unit:

    def __init__(self, c, v=0):
        self.c, self.v, self.r = c, v, c % SETS

    def at(self, d):
        return self.v * SETS + (self.c + d)

    def full(self):
        return self.v * 16 + 16 * (self.c // SETS + 1)


class Tally:

    def __init__(self, sem):
        self.sem, self.n, self.v = sem, 0, 0

    def up(self, ins):
        ins.then_inc(self.sem, 1)
        self.n += 1

    def wait(self, eng):
        eng.wait_ge(self.sem, self.v + self.n)


def program(nc, A, out, stages=ORDER):
    base, n_units = {}, 0
    for name in stages:
        base[name] = n_units
        n_units += STAGE_UNITS[name]
    ctx = ExitStack()

    def sb(name, shape, dt=F32):
        return ctx.enter_context(nc.sbuf_tensor(name, shape, dt))

    def sb_both(name, shape):
        with nc.sbuf_tensor(name + "_r", shape, F32R) as rounded:
            pass
        return sb(name, shape), rounded

    def sem(name):
        return ctx.enter_context(nc.semaphore(name))

    ring, ring_r = sb_both("ring", [P, 2 * SETS, 11 * COLS])
    xT = sb("xT", [P, KD, T])
    hT, hT_r = sb_both("hT", [P, KD, T])
    sq, sq_r = sb_both("sq", [P, KD, T])
    act, act_r = sb_both("act", [P, KF, T])
    store_area, store_area_r = sb_both("store_area", [P, 72 * T])
    arena = store_area[:, 0:64 * T]
    ptmp, rs = store_area[:, 64 * T:68 * T], store_area[:, 68 * T:72 * T]
    silu_g = sb("silu_g", [P, SETS, 2 * T])
    gla_w2 = sb("gla_w2", [16, T])
    ramp = sb("ramp", [P, T])
    window = sb("window", [P, 64])
    parity = sb("parity", [P, 10])
    s5c = sb("s5c", [P, 4, 32])
    router = sb("router", [P, KD, E_EXP])
    route = sb("route", [P, 16, 10])
    route_u = sb("route_u", [P, 2, E_EXP], U32)
    counts = sb("counts", [1, E_EXP], I32)
    qn_col = sb("qn_col", [P, 1])
    row_max = sb("row_max", [P, 2, 2])
    row_sum = sb("row_sum", [P, 2, 2])
    row_inv = sb("row_inv", [P, 2, 2])
    std = sb("std", [P, 4 * T])
    ident = sb("ident", [P, P])
    ones = sb("ones", [P, T])
    mirror = sb("mirror", [P, P])
    halves = sb("halves", [P, P])
    causal = sb("causal", [P, 3, P])
    upper = sb("upper", [P, 3, P])
    lower = sb("lower", [P, 3, P])
    vrows = sb("vrows", [P, 5, P])
    vc = sb("vc", [P, 5, P])
    mods = sb("mods", [P, 4, 24])
    gains = sb("gains", [P, 4, KD])
    c_raw_cols = sb("c_raw_cols", [P, KD])
    csil = sb("csil", [P, KD])
    small = sb("small", [P, 128])
    banks = [ctx.enter_context(nc.psum_tensor(f"bank{i}", [P, 512], F32)) for i in range(8)]
    bank_sum, bank_x = banks[7], banks[6]

    slot_full = [sem(f"slot_full{i}") for i in range(2 * SETS)]
    unit_done = sem("unit_done")
    evac = sem("evac")
    silu_ready = sem("silu_ready")
    sq_ready, sum_ready, std_ready, h_ready = (sem(s) for s in ("sq_ready", "sum_ready", "std_ready", "h_ready"))
    x_ready = sem("x_ready")
    scaled = sem("scaled")
    const_ready = sem("const_ready")
    vec_in = sem("vec_in")
    x_in, c_in = sem("x_in"), sem("c_in")
    x_tr = sem("x_tr")
    vec_tr = sem("vec_tr")
    vec_ready = sem("vec_ready")
    csil_ready = sem("csil_ready")
    mod_ready = sem("mod_ready")
    mod_dve = sem("mod_dve")
    mod_pool = sem("mod_pool")
    out_tr, out_cp, out_done = sem("out_tr"), sem("out_cp"), sem("out_done")
    cols_in = sem("cols_in")
    (prm_in, s5_dt, s5_expo, s5_mag, s5_red, s5_sin, s5_rows, s5_tr, s5_cols, range_ready, sin_ready, tab_ready, raw_in,
     b_zero, b_exp, c_exp, bc_tr, bc_cp) = (sem(n) for n in (
        "prm_in", "s5_dt", "s5_expo", "s5_mag", "s5_red", "s5_sin", "s5_rows", "s5_tr", "s5_cols", "range_ready",
        "sin_ready", "tab_ready", "raw_in", "b_zero", "b_exp", "c_exp", "bc_tr", "bc_cp"))
    bu_ready, bu_turned, turned, scanned, back_c, w_ready, w_used, y_ready, y_read, y_gelu, glu_sig = (
        sem(n) for n in ("bu_ready", "bu_turned", "turned", "scanned", "back_c", "w_ready", "w_used", "y_ready", "y_read",
                         "y_gelu", "glu_sig"))
    (logit_ready, tok_tr, tok_cp, gap_ready, gap_exp, mask_ready, pos_ready, routed, pick_ready, pick_tr, pick_cp, gathered,
     gather_cp, scattered, scatter_read) = (sem(n) for n in (
        "logit_ready", "tok_tr", "tok_cp", "gap_ready", "gap_exp", "mask_ready", "pos_ready", "routed", "pick_ready",
        "pick_tr", "pick_cp", "gathered", "gather_cp", "scattered", "scatter_read"))
    (dt_x, dt_soft, dt_ready, a_exp, dt_tr, dt_cols, pads, conv_in, conv_done, xs_ready, xs_tr, xdt_ready, cb_ready, cb_masked,
     rows_ready, rows_read, seg_ready, decay_exp, weights_f, weights_b, pair_ready, pair_read, y_gated, y_sq, y_sum, y_std,
     y_normed) = (sem(n) for n in (
        "dt_x", "dt_soft", "dt_ready", "a_exp", "dt_tr", "dt_cols", "pads", "conv_in", "conv_done", "xs_ready", "xs_tr",
        "xdt_ready", "cb_ready", "cb_masked", "rows_ready", "rows_read", "seg_ready", "decay_exp", "weights_f", "weights_b",
        "pair_ready", "pair_read", "y_gated", "y_sq", "y_sum", "y_std", "y_normed"))
    rpb_in, qk_raw, qk_sq, qk_sum, qk_std, qk_ready = (
        sem(n) for n in ("rpb_in", "qk_raw", "qk_sq", "qk_sum", "qk_std", "qk_ready"))
    down_freed = sem("down_freed")
    p_in, p_tr, p_cp, post_sq, post_sum, post_std = (sem(n) for n in ("p_in", "p_tr", "p_cp", "post_sq", "post_sum", "post_std"))
    gate_x = sem("gate_x")
    gate_w = sem("gate_w")
    decay_ps, decay_x, soft_ready = sem("decay_ps"), sem("decay_x"), sem("soft_ready")
    cum_ready = sem("cum_ready")
    key_raw, key_exp, key_ready, key_used = sem("key_raw"), sem("key_exp"), sem("key_ready"), sem("key_used")
    query_raw, query_exp, query_ready = sem("query_raw"), sem("query_exp"), sem("query_ready")
    gla_scores, gla_masked, gla_out, gla_sq, gla_sum, gla_std, gla_done = (
        sem(n) for n in ("gla_scores", "gla_masked", "gla_out", "gla_sq", "gla_sum", "gla_std", "gla_done"))
    score_ready, score_max, prob_exp, prob_ready, prob_tr, prob_cp, head_out, heads_read = (
        sem(n) for n in ("score_ready", "score_max", "prob_exp", "prob_ready", "prob_tr", "prob_cp", "head_out", "heads_read"))
    xg_low, hid_turned, hid_high, hid_low = (sem(n) for n in ("xg_low", "hid_turned", "hid_high", "hid_low"))
    w_high, w_low, h_high, h_low, act_high, act_low = (
        sem(n) for n in ("w_high", "w_low", "h_high", "h_low", "act_high", "act_low"))
    v_chain, a_chain, p_chain = sem("v_chain"), sem("a_chain"), sem("p_chain")

    def w3(name, *idx):
        a = A[name]
        for i in idx:
            a = a[i]
        return a.rearrange("(k p) m -> p k m", p=P)

    ROWS = [
        [("e_norm_mix", 8), ("e_norm_ffn", 8), ("o_norm_mix", 8), ("o_norm_ffn", 8), ("ffn1_norm_2", 16),
         ("mix_norm_2", 16), ("ffn2_norm_2", 16), ("ple_norm_2", 16), ("ple_post_norm_2", 16), ("o_d_skip", 8)],
        [("ssd_norm_2", 16), ("ssd_conv_b_2", 48), ("e_gla_b2", 2), ("e_gla_norm", 1), ("final_norm", 8)],
        [("e_mod_mix_b", 24), ("e_mod_ffn_b", 24), ("o_mod_mix_b", 24), ("o_mod_ffn_b", 24)],
    ]
    where, vec_loads = {}, []
    for t, rows in enumerate(ROWS):
        r = 0
        for name, n in rows:
            where[name] = (t, r)
            a = A[name]
            vec_loads.append((vrows[r:r + n, t, :],
                              (a if len(a.shape) == 1 else a.rearrange("a b -> (a b)")).rearrange("(r q) -> r q", q=P)))
            r += n
    QN_ROW, KN_ROW = 75, 76
    VEC_ROWS = (120, 77, 96, 120, 120)
    for row, name in ((QN_ROW, "na_q_norm_2"), (KN_ROW, "na_k_norm_2")):
        for half in range(2):
            vec_loads.append((vrows[row:row + 1, 1, 64 * half:64 * half + 64], A[name]))
    taps = A["ssd_conv_w_2"][0].rearrange("t (j q) -> (t j) q", q=P)
    for half in range(2):
        vec_loads.append((vrows[0:120, 3 + half, :], taps[120 * half:120 * half + 120, :]))

    def vcol(name, j, n=1):
        t, r = where[name]
        return vc[:, t, r + j:r + j + n]

    def conv_col(tap, j):
        r = tap * 48 + j
        return vc[:, 3 + r // 120, r % 120:r % 120 + 1]

    NORMS = {}

    def norm_entry(name, needs, gain, shift=None):
        if needs in stages:
            NORMS[name] = (len(NORMS), gain, shift)

    for name, needs, m in (("em", "even_in", 0), ("ef", "even_ffn", 1), ("om", "s5_in", 2), ("of", "moe", 3)):
        norm_entry(name, needs, lambda k, m=m: gains[:, m, k:k + 1], lambda k, m=m: mods[:, m, k:k + 1])
        if name == "of":
            norm_entry("final", "final", lambda k: vcol("final_norm", k))
    for i in range(2):
        for name, needs, vec in ((f"ffn1_{i}", f"ffn1_{i}", "ffn1_norm_2"), (f"mix_{i}", ("ssd_in", "na_in")[i], "mix_norm_2"),
                                 (f"ffn2_{i}", f"ffn2_{i}", "ffn2_norm_2"), (f"ple_{i}", f"ple_{i}", "ple_norm_2")):
            norm_entry(name, needs, lambda k, i=i, vec=vec: vcol(vec, 8 * i + k))

    H_BEFORE = {name: n - (name != "final" and "final" in NORMS and n > NORMS["final"][0])
                for name, (n, _, _) in NORMS.items()}

    def x_whole():
        head = {}
        at, now, nx, blocks = {}, (x_ready, 1), 1, KD - 2
        before = dict(even_in="em", even_ffn="ef", s5_in="om", moe="of", final="final", ffn1_0="ffn1_0", ssd_in="mix_0",
                      ffn2_0="ffn2_0", ple_0="ple_0", ffn1_1="ffn1_1", na_in="mix_1", ffn2_1="ffn2_1", ple_1="ple_1")
        for s in stages:
            if s in before:
                at[before[s]], head[before[s]] = now, blocks
            if s == "moe":
                now, blocks = (scatter_read, 1 + 4 * E_EXP), KD - 2
            if s in ("even_out", "even_ffn", "s5_out", "ffn1_0", "ssd_out", "ffn2_0", "ffn1_1", "na_out", "ffn2_1"):
                now = (evac, base[s] + STAGE_UNITS[s])
                blocks = KD - 4 if s in ("even_out", "s5_out", "na_out") else KD - 2
            if s in ("final", "ple_0", "ple_1"):
                nx += 1
                now = (x_ready, nx)
        at["end"] = now
        return at, head

    X_AT, X_HEAD = x_whole()


    def slot(u, s, kk, rounded=False):
        return (ring_r if rounded else ring)[:, 2 * u.r + s, 0:kk * COLS].rearrange("p (k m) -> p k m", m=COLS)

    def repeat(eng, first, count, body, outer=0):
        done = 0
        if count >= 2 * SETS and first >= SETS:
            loops = count // SETS
            with eng.Fori(0, loops) as it:
                for c in range(SETS):
                    body(Unit(first + c, it + outer), it * SETS + c)
            done = loops * SETS
        for c in range(done, count):
            body(Unit(first + c, outer), c)

    def area(first, n, width=T):
        return arena[:, first * T:(first + n) * T].rearrange("p (k t) -> p k t", t=width)

    has = lambda name: name in stages

    EPS_COL, FB_COL, DTB_COL, ALOG_COL = 0, 1, 2, 3
    COL_LOADS = [(small[0:8, FB_COL:FB_COL + 1], A["e_fox_fb"].rearrange("a n -> n a"))]
    COL_LOADS += [(small[32 * d:32 * d + 32, c:c + 1], A[n][0, d:d + 1, :].rearrange("a n -> n a"))
                  for c, n in ((DTB_COL, "ssd_dt_bias_2"), (ALOG_COL, "ssd_a_log_2")) for d in range(2)]

    DH = 64
    fox_q, fox_k, fox_v = area(0, 4), area(4, 4), area(8, 4, 2 * T)
    gla_q, gla_k, gla_v, gla_g = area(12, 2), area(14, 2), area(16, 4, 2 * T), area(20, 4)
    gla_b, gla_qd = area(24, 2), area(26, 2)
    gla_kd = area(28, 6)
    gla_a = area(34, 6, 3 * P)
    gla_o, gla_osq = area(40, 4), area(44, 4)
    gate_in, gate_low, soft = area(48, 3), area(51, 1), area(52, 3)
    fox_cum = area(55, 1)
    EVEN = [(1536, 8, 3080, 16), (1544, COLS, 1800, COLS), (2056, COLS, 2312, COLS), (0, COLS, 256, COLS),
            (512, COLS, 768, COLS), (1024, COLS, 1280, COLS), (2568, COLS, 2824, COLS)]
    GB = 32
    NB = T // GB

    probs, probsT = area(56, 4, 2 * T), area(60, 4, 2 * T)

    p_tok, pT = act[:, 16:18, :], act[:, 18:20, :]

    class Attention:

        def __init__(self, first, heads, q, k, v, out, widths, mask, bias):
            self.first, self.heads, self.q, self.k, self.v, self.out = first, heads, q, k, v, out
            self.widths, self.mask, self.bias = widths, mask, bias

        def part(self, h):
            return slice(DH * (h % 2), DH * (h % 2) + DH)

        def span(self, a):
            return slice(self.widths[0] * a, self.widths[0] * a + self.widths[a])

    FOX = Attention(0, 8, fox_q, fox_k, fox_v, lambda j: act[:, j, :], (P, T),
                    lambda h, a: causal[:, 1, :] if a == 0 else causal[:, 0:2, :].rearrange("p a t -> p (a t)"),
                    lambda h, a: (ident[0:8, h:h + 1].to_broadcast([8, P]), fox_cum[0:8, 0, 0:T if a else P]))
    n_fox = 8 if has("even_in") else 0

    NS = 32
    s5_cos, s5_sin_t = area(0, NS), area(NS, NS)

    def prm(n, w=P):
        return act[0:NS, 10 + n // 2, (n % 2) * P:(n % 2) * P + w]
    TWO_PI_A = 6.28125
    TWO_PI_B = 2.0 * math.pi - TWO_PI_A
    MAGIC = 1.5 * 2.0 ** 23
    PI_IN = 3.1415925
    flat2 = lambda t: t.rearrange("p k t -> p (k t)")
    b_raw = [flat2(act[:, 8:10, :]).rearrange("p (i k) -> p i k", k=16), flat2(act[:, 10:12, :]).rearrange("p (i k) -> p i k", k=16)]
    c_raw = [flat2(act[:, 20:22, :]).rearrange("p (m q) -> p m q", q=64), std[:, 2 * T:4 * T].rearrange("p (m q) -> p m q", q=64)]
    b_wide = [flat2(act[:, 12 + 4 * n:16 + 4 * n, :]).rearrange("p (i k) -> p i k", k=32) for n in range(2)]
    c_wide = [flat2(act[:, 12 + 4 * n:16 + 4 * n, :]).rearrange("p (m j q) -> p m j q", j=2, q=64) for n in range(2)]
    bT = [flat2(sq[:, 4 * n:4 * n + 4, :]).rearrange("p (m s) -> p m s", s=P) for n in range(2)]
    cT = [flat2(hT[:, 4 * n:4 * n + 4, :]).rearrange("p (m s) -> p m s", s=P) for n in range(2)]
    s5_t1 = [silu_g[:, n, :].rearrange("p (c t) -> p c t", c=2) for n in range(2)]
    s5_t2 = [ptmp[:, 2 * T * n:2 * T * (n + 1)].rearrange("p (c t) -> p c t", c=2) for n in range(2)]
    s5_z = [std[:, 2 * T * n:2 * T * (n + 1)].rearrange("p (c t) -> p c t", c=2) for n in range(2)]
    s5_u1 = [rs[:, 2 * T * n:2 * T * (n + 1)].rearrange("p (c t) -> p c t", c=2) for n in range(2)]
    s5_u2 = [act[:, 16 + 2 * n:18 + 2 * n, :] for n in range(2)]

    h_tok = sq[:, :, :].rearrange("p k t -> p (k t)").rearrange("p (a d) -> p a d", a=2)
    xg = area(0, 8)
    yg = area(8, 8, D)
    pick, pick_w, pick_t = area(16, 2), area(18, 2), area(20, 2)
    ramp1 = area(22, 1)
    xg_r = store_area_r[:, 0:8 * T].rearrange("p (k t) -> p k t", t=T)
    HIGH, LOW = slice(0, P), slice(P, T)
    MOE_HIGH = 23
    HIDDEN = slice(T, 2 * T)
    LOGIT, TOP, TOPI, GATE, CHOSEN, POS, MISC = 0, 2, 4, 6, 8, 10, 12

    NH = 32
    ssd_seg = [[flat2(area(48, 6)), flat2(area(54, 6))], [flat2(hT[:, 0:6, :]), flat2(act[:, 16:22, :])]]
    ssd_cb = [[t[:, 3 * P * d:3 * P * (d + 1)] for d in range(2)] for t in (std, rs)]
    ssd_x = [[flat2(sq[:, 4 * b + 2 * d:4 * b + 2 * d + 2, :]).rearrange("p (s f) -> p s f", s=2) for d in range(2)] for b in range(2)]
    run_rows, dt_rows = area(60, 1), area(61, 1)
    run_cols = flat2(area(62, 1))[:, 0:P].rearrange("p (s r) -> p s r", s=2)
    dt_cols_t = flat2(area(62, 1))[:, P:2 * P].rearrange("p (s r) -> p s r", s=2)
    d_cols = small[:, 16:32]
    d_rows = sb("d_rows", [16, P + 2])
    conv_buf = silu_g[:, :, :].rearrange("p r t -> p (r t)")[:, 0:4 * 260].rearrange("p (j t) -> p j t", t=260)

    na_q, na_k, na_v = area(0, 8), area(8, 8), area(16, 8, D)
    na_bias = flat2(area(24, 24)).rearrange("p (h r c) -> p h r c", h=16, c=64)
    NA = Attention(n_fox, 16, na_q, na_k, na_v, lambda j: act[:, j, :], (T, T),
                   lambda h, a: window[:, :].rearrange("p (b c) -> p b c", b=1).to_broadcast([P, 4, 64]),
                   lambda h, a: (mirror[:, :], na_bias[:, h, 2 - 2 * a:6 - 2 * a, :].rearrange("p r c -> p (r c)")))

    SPLIT = [s for s in stages if s[:5] in ("ffn1_", "ffn2_")]
    h_hi, h_lo, act_lo = sq_r, hT_r, act_r

    def high_area(first, n):
        return store_area_r[:, first * T:(first + n) * T].rearrange("p (k t) -> p k t", t=T)
    act_hi = high_area(48, KF)
    as_f = lambda ap: ap.bitcast(F32)

    def gate_up_high(stage, u, s):
        last = (base[stage] + GU_UNITS - 1) % SETS
        return high_area((MOE_HIGH if stage == "moe" else 0) + 16 * ((u.r - last - 1) % SETS) + KD * s, KD)

    def down_high(i, s, stage=None):
        return high_area((MOE_HIGH if stage == "moe" else 0) + 24 * (i % 2) + 11 * s, 11)

    def slots_before(stage, i):
        if stage == "moe":
            return i * 2
        return (i + (SPLIT.index(stage) * STAGE_UNITS[stage] + (STAGE_UNITS["moe"] if has("moe") else 0))) * 2

    def next_unit(u):
        return Unit(u.c + 1, u.v)

    MOD_STEPS = 2 * KD
    em_parts = lambda i: area(2 * i, 2)
    ef_parts = lambda i: sq[:, 2 * (i % 4):2 * (i % 4) + 2, :]
    ffn_mod_parts = lambda i: sq[:, 2 * i:2 * i + 2, :]
    EF_AT = {1: 0, 2: 1, 3: 2, 6: 3, 7: 4, 8: 5}
    ef_bank = lambda i: (bank_x, bank_sum)[i % 2]

    def mod_weights(name):
        return A[name][0].rearrange("(p k) m -> p k m", p=P)

    def mod_in_ffn(eng, first, gate_up, modulation, down, early=lambda *a: None):
        def both(layer, u, i, *mod):
            early(*mod)
            layer(u, i)
            modulation(*mod)

        gate_up(Unit(first), 0)
        with eng.Fori(0, 2) as it:
            for c in range(3):
                both(gate_up, Unit(first + 1 + 2 * c, it * 2), it * 3 + (c + 1), Unit(first + 2 + 2 * c, it * 2), 0, it * 3 + c, c)
        n = first + 13
        for c in range(3):
            both(gate_up, Unit(n + 2 * c), 7 + c, Unit(n + 1 + 2 * c), 1, c, c)
        n += 6
        gate_up(Unit(n), 10)
        for i in range(3):
            both(down, Unit(n + 1 + 2 * i), i, Unit(n + 2 + 2 * i), 1, 3 + i, i)
        down(Unit(n + 7), 3)

    def by_count(eng, expert):
        with eng.Fori(0, E_EXP) as e:
            n = eng.value_load(counts[0:1, bass.ds(e, 1)], min_val=0, max_val=T)
            with eng.If(n > P):
                expert(e, T)
            with eng.Else():
                expert(e, P)

    with nc.Block() as block:

        @block.sync
        def _(sp):
            sp.dma_start(c_raw_cols[:, :], A["c"].rearrange("a (p k) -> p (a k)", p=P)).then_inc(c_in, 16)
            sp.dma_start(sq[:, :, :].rearrange("p k t -> p (k t)").rearrange("p (a d) -> p a d", a=2),
                         A["x"][0].rearrange("(a p) d -> p a d", p=P)).then_inc(x_in, 16)

            def load(u, s, src):
                kk, m = src.shape[1], src.shape[2]
                sp.dma_start(slot(u, s, kk)[:, :, 0:m], src).then_inc(slot_full[2 * u.r + s], 16)

            def small_loads():
                for dst, src in vec_loads[::2]:
                  sp.dma_start(dst, src).then_inc(vec_in, 16)
                for dst, src in COL_LOADS:
                  sp.dma_start(dst, src).then_inc(cols_in, 16)
                sp.dma_start(gla_w2[:, :], A["e_gla_w2"][0]).then_inc(cols_in, 16)
                sp.dma_start(d_rows[:, P:P + 2], A["ssd_d_2"].rearrange("a (j g) -> j (a g)", g=2)).then_inc(cols_in, 16)
                sp.dma_start(router[:, :, :], w3("o_router", 0)).then_inc(cols_in, 16)
                if has("s5_prep"):
                    for n, name in enumerate(("o_lam_re", "o_lam_im")):
                        sp.dma_start(prm(n), A[name][0].rearrange("(i g) q -> i (g q)", g=2)).then_inc(prm_in, 16)
                    sp.dma_start(prm(2, 2), A["o_log_dt"].rearrange("a (i g) -> i (a g)", g=2)).then_inc(prm_in, 16)

            def freed(u):
                if u.c >= SETS or not isinstance(u.v, int):
                    sp.wait_ge(unit_done, u.at(1 - SETS))

            def columns(stage, w, count=None, first=0):
                def body(u, i):
                    freed(u)
                    for s in range(2):
                        load(u, s, w[:, :, bass.ds(i * (2 * COLS) + s * COLS, COLS)])
                if stage == "mod_em":
                    for i in range(6):
                        if i == SETS:
                            small_loads()
                        body(Unit(i), i)
                    return
                repeat(sp, base[stage] + first, count or STAGE_UNITS[stage], body)

            def rows_halved_unit(u, w, i):
                half = w.shape[1] // 2
                freed(u)
                for s in range(2):
                    load(u, s, w[:, s * half:(s + 1) * half, i * COLS:(i + 1) * COLS])

            def rows_halved(first, w, count):
                for i in range(count):
                    rows_halved_unit(Unit(first + i), w, i)

            def even_ffn():
                def gate_up(u, i):
                    freed(u)
                    for s, name in enumerate(("e_ffn_gate", "e_ffn_up")):
                        load(u, s, w3(name, 0)[:, :, bass.ds(i * COLS, COLS)])

                def modulation(u, which, i, place):
                    freed(u)
                    for s in range(2):
                        load(u, s, mod_weights(("o_mod_mix_w", "o_mod_ffn_w")[which])[:, :, bass.ds(i * (2 * COLS) + s * COLS, COLS)])
                mod_in_ffn(sp, base["even_ffn"], gate_up, modulation,
                           lambda u, i: rows_halved_unit(u, w3("e_ffn_down", 0), i))

            def ffn(stage, w_gate, w_up, w_down):
                def body(u, i):
                    freed(u)
                    for s, w in enumerate((w_gate, w_up)):
                        load(u, s, w[:, :, bass.ds(i * COLS, COLS)])
                repeat(sp, base[stage], GU_UNITS, body)
                rows_halved(base[stage] + GU_UNITS, w_down, DN_UNITS)

            def ffn2(stage, name, i):
                gu = w3(f"{name}_w_gu_2", i)
                ffn(stage, gu[:, :, 0:FF], gu[:, :, FF:2 * FF], w3(f"{name}_w_down_2", i))

            MODW = dict(mod_em="e_mod_mix_w", mod_ef="e_mod_ffn_w")
            for stage in stages:
                if stage in MODW:
                    columns(stage, mod_weights(MODW[stage]))
                if stage == "even_in":
                    w = w3("e_w_in", 0)
                    for i, (c0, n0, c1, n1) in enumerate(EVEN):
                        u = Unit(base[stage] + i)
                        freed(u)
                        load(u, 0, w[:, :, c0:c0 + n0])
                        load(u, 1, w[:, :, c1:c1 + n1])
                if stage == "even_out":
                    columns(stage, w3("e_w_o", 0))
                if stage == "even_ffn":
                    even_ffn()
                if stage in ("s5_in", "s5_glu", "s5_out"):
                    columns(stage, w3(dict(s5_in="o_w_in", s5_glu="o_w_glu", s5_out="o_w_o")[stage], 0))
                if stage == "moe":
                    first = base[stage]
                    kinds = [A[n][0].rearrange("e (k p) m -> e p k m", p=P) for n in ("o_exp_gate", "o_exp_up", "o_exp_down")]
                    with sp.Fori(0, E_EXP) as e:
                        def expert_columns(n, col, rows=slice(0, KF)):
                            return kinds[n][bass.ds(e, 1), :, rows, col].rearrange("a p k m -> p (a k) m")

                        def body(u, i):
                            freed(u)
                            for s in range(2):
                                load(u, s, expert_columns(s, bass.ds(i * COLS, COLS), slice(0, KD)))
                        repeat(sp, first, GU_UNITS, body, outer=e * 5)
                        for i in range(DN_UNITS):
                            u = Unit(first + GU_UNITS + i, e * 5)
                            freed(u)
                            sp.sem_inc(down_freed, 1)
                            for s in range(2):
                                load(u, s, expert_columns(2, slice(i * COLS, (i + 1) * COLS), slice(11 * s, 11 * s + 11)))
                if stage == "ssd_in":
                    w = w3("ssd_w_in_2", 0)
                    u = Unit(base[stage])
                    freed(u)
                    for s in range(2):
                        load(u, s, w[:, :, 8192 + NH * s:8192 + NH * (s + 1)])
                    columns(stage, w, 16, first=1)
                if stage == "ssd_out":
                    rows_halved(base[stage], w3("ssd_w_out_2", 0), 4)
                if stage == "na_in":
                    columns(stage, w3("na_w_qkv_2", 0))
                if stage == "na_out":
                    columns(stage, w3("na_w_out_2", 0))
                if stage[:5] in ("ffn1_", "ffn2_"):
                    ffn2(stage, stage[:4], int(stage[5]))
                if stage[:4] == "ple_":
                    columns(stage, w3("ple_w_gate_2", int(stage[4])), 2)
                    columns(stage, w3("ple_w_proj_2", int(stage[4])), 2, first=2)

            sp.wait_ge(cols_in, 16 * (len(COL_LOADS) + 3))
            if has("moe"):
                sp.wait_ge(down_freed, E_EXP * DN_UNITS)
            sp.wait_ge(out_cp, 4)
            sp.dma_start(out[0].rearrange("(a p) d -> p a d", p=P),
                         sq[:, :, :].rearrange("p k t -> p (k t)").rearrange("p (a d) -> p a d", a=2)).then_inc(out_done, 16)
            sp.wait_ge(out_done, 16)

        @block.gpsimd
        def _(pool):
            tally = Tally(p_chain)

            def fill(t, value):
                tally.up(nc.gpsimd.memset(t, value))

            def select(t, op, value, step, mult, offset=0):
                tally.wait(pool)
                tally.up(nc.gpsimd.affine_select(out=t, in_=t, compare_op=op, fill=value, base=offset,
                                                 pattern=[[step, t.shape[-1]]], channel_multiplier=mult))

            fill(ident[:, :], 0.0)
            fill(ones[:, :], 1.0)
            fill(halves[:, :], 0.0)
            fill(causal[:, :, :], 0.0)
            fill(mirror[:, :], 0.0)
            fill(upper[:, :, :], 1.0)
            fill(lower[:, :, :], 1.0)
            tally.wait(pool)
            fill(halves[0:64, 0:64], 1.0)
            fill(halves[64:128, 64:128], 1.0)
            select(ident[:, :], ALU.not_equal, 1.0, -1, 1)
            for total in (63, 191):
                select(mirror[:, :], ALU.not_equal, 1.0, 1, 1, -total)
            select(causal[:, 1, :], ALU.is_ge, NEG, -1, 1)
            for i in (0, 2):
                select(upper[:, i, :], ALU.is_ge, 0.0, 1, -1)
                select(lower[:, i, :], ALU.is_ge, 0.0, -1, 1)
            fill(window[:, :], 0.0)
            fill(parity[:, 2:10], 1.0)
            for half in range(2):
                part = window[64 * half:64 * half + 64, :]
                select(part[:, 0:48], ALU.is_ge, NEG, 1, -1, 8)
                select(part[:, 16:64], ALU.is_ge, NEG, -1, 1, 7 - 16)
            select(parity[:, 2:10], ALU.is_ge, 0.0, -16, 1)
            select(parity[:, 2:10], ALU.is_ge, 0.0, 16, -1, 15)
            tally.up(nc.gpsimd.iota(ptmp[:, 0:T].bitcast(I32), pattern=[[1, T]], base=0, channel_multiplier=0))
            tally.wait(pool)
            tally.up(nc.gpsimd.tensor_copy(ramp[:, :], ptmp[:, 0:T].bitcast(I32)))
            tally.wait(pool)
            nc.gpsimd.memset(small[:, 0:1], EPS).then_inc(const_ready, 1)

            def s5_angles():
                pool.wait_ge(s5_cols, 1)
                for c in range(NS // 2):
                    r, r2 = s5_cos[:, 2 * c:2 * c + 2, :], flat2(s5_cos[:, 2 * c:2 * c + 2, :])
                    k, m = ptmp[:, 0:2 * T], ptmp[:, 2 * T:4 * T]
                    for j in range(2):
                        tally.up(nc.gpsimd.tensor_scalar(r[:, j, :], ramp[:, :], s5c[:, 1, 2 * c + j:2 * c + j + 1], None, ALU.mult))
                    tally.wait(pool)
                    tally.up(nc.gpsimd.tensor_scalar(k, r2, 0.5 / math.pi, MAGIC, ALU.mult, ALU.add))
                    tally.wait(pool)
                    tally.up(nc.gpsimd.tensor_scalar(k, k, MAGIC, None, ALU.subtract))
                    for part in (TWO_PI_A, TWO_PI_B):
                        tally.wait(pool)
                        tally.up(nc.gpsimd.tensor_scalar(m, k, part, None, ALU.mult))
                        tally.wait(pool)
                        tally.up(nc.gpsimd.tensor_tensor(r2, r2, m, ALU.subtract))
                    tally.wait(pool)
                    nc.gpsimd.tensor_scalar(r2, r2, PI_IN, -PI_IN, ALU.min, ALU.max).then_inc(range_ready, 1)

            def s5_cosines():
                for c in range(NS // 4):
                    pool.wait_ge(sin_ready, c + 1)
                    t = s5_cos[:, 4 * c:4 * c + 4, :]
                    tally.up(nc.gpsimd.tensor_tensor(t, t, t, ALU.mult))
                    tally.wait(pool)
                    nc.gpsimd.tensor_scalar(t, t, -2.0, 1.0, ALU.mult, ALU.add).then_inc(tab_ready, 1)

            def s5_main():
                pool.wait_ge(raw_in, 64)
                tally.up(nc.gpsimd.memset(b_wide[0], 0.0))
                nc.gpsimd.memset(b_wide[1], 0.0).then_inc(b_zero, 1)
                for i in range(NS + 1):
                    if i < NS:
                        pool.wait_ge(bu_turned, i + 1)
                        t1, t2 = s5_t1[i % 2], s5_t2[i % 2]
                        nc.gpsimd.tensor_tensor(t1[:, 0, :], t1[:, 0, :], t2[:, 1, :], ALU.add)
                        nc.gpsimd.tensor_tensor(t1[:, 1, :], t1[:, 1, :], t2[:, 0, :], ALU.subtract).then_inc(turned, 1)
                    if i >= 1:
                        j = i - 1
                        pool.wait_ge(scanned, j + 1)
                        u1, u2 = s5_u1[j % 2], s5_u2[j % 2]
                        tally.up(nc.gpsimd.tensor_tensor(u2, s5_z[j % 2], s5_sin_t[:, j:j + 1, :].to_broadcast([P, 2, T]), ALU.mult))
                        tally.wait(pool)
                        pool.wait_ge(back_c, j + 1)
                        nc.gpsimd.tensor_tensor(u1[:, 0, :], u1[:, 0, :], u2[:, 1, :], ALU.subtract)
                        nc.gpsimd.tensor_tensor(u1[:, 1, :], u1[:, 1, :], u2[:, 0, :], ALU.add).then_inc(w_ready, 1)

            def ssd():
                for g in range(9):
                    if g < 8:
                        pool.wait_ge(decay_exp, 2 * g + 2)
                        pool.wait_ge(cb_masked, 2 * g + 2)
                        seg = ssd_seg[g % 2][1].rearrange("p (h t) -> p h t", h=4)
                        cb = ssd_cb[g % 2][1].rearrange("p (a t) -> p a t", a=1).to_broadcast([P, 4, 3 * P])
                        nc.gpsimd.tensor_tensor(seg, seg, cb, ALU.mult).then_inc(weights_b, 1)
                    if g >= 1:
                        j = g - 1
                        pool.wait_ge(pair_read, 2 * j + 2)
                        y = arena[:, 2 * j * T:(2 * j + 2) * T].rearrange("p (k t) -> p k t", t=T)
                        nc.gpsimd.tensor_tensor(y, y, act[:, 2 * j:2 * j + 2, :], ALU.mult).then_inc(y_gated, 1)

            def mod_ef():
                for i in range(6):
                    u = Unit(base["mod_ef"] + i)
                    if i == 0:
                        pool.wait_ge(sum_ready, 1)
                    if i >= 4:
                        pool.wait_ge(unit_done, base["mod_ef"] + i - 3)
                    for s in range(2):
                        w = slot(u, s, KD)
                        pool.wait_ge(slot_full[2 * u.r + s], u.full())
                        tally.up(nc.gpsimd.tensor_tensor(w, w, csil[:, :].rearrange("p (k m) -> p k m", m=1).to_broadcast([P, KD, COLS]),
                                                         ALU.mult))
                        for n in (4, 2):
                            tally.wait(pool)
                            tally.up(nc.gpsimd.tensor_tensor(w[:, 0:n, :], w[:, 0:n, :], w[:, n:2 * n, :], ALU.add))
                        tally.wait(pool)
                        nc.gpsimd.tensor_tensor(ef_parts(i)[:, s, :], w[:, 0, :], w[:, 1, :], ALU.add).then_inc(mod_pool, 1)

            for stage in stages:
                if stage == "mod_ef":
                    mod_ef()
                if stage == "s5_prep":
                    s5_angles()
                if stage == "s5_tab":
                    s5_cosines()
                if stage == "s5_in":
                    s5_main()
                if stage == "ssd_in":
                    ssd()

        @block.tensor
        def _(pe):
            mm = nc.tensor.matmul
            pe.wait_ge(const_ready, 1)
            pe.wait_ge(x_in, 16)
            x_tok = sq[:, :, :].rearrange("p k t -> p (k t)").rearrange("p (a d) -> p a d", a=2)
            for b in range(4):
                for j in range(2):
                    k = 2 * b + j
                    for a in range(2):
                        i = nc.tensor.transpose(banks[b][:, j * T + a * P:j * T + (a + 1) * P],
                                                x_tok[:, a, k * P:(k + 1) * P], ident[:, :])
                i.then_inc(x_tr, 1)
            pe.wait_ge(vec_in, 16 * len(vec_loads))
            for t in range(5):
                n = VEC_ROWS[t]
                i = nc.tensor.transpose((bank_x if t < 4 else bank_sum)[:, (t % 4) * P:(t % 4) * P + n],
                                        vrows[0:n, t, :], ident[0:n, 0:n])
            i.then_inc(vec_tr, 1)

            def banks_free(u):
                if u.c >= SETS or not isinstance(u.v, int):
                    pe.wait_ge(evac, u.at(1 - SETS))

            def wide(u, kk, rhs, ready=None):
                banks_free(u)
                for s in range(2):
                    pe.wait_ge(slot_full[2 * u.r + s], u.full())
                    w = slot(u, s, kk)
                    for t in range(2):
                        for k in range(kk):
                            if ready and s == t == 0:
                                ready(k)
                            i = mm(banks[2 * u.r + s][:, t * T:(t + 1) * T], w[:, k, t * P:(t + 1) * P], rhs(k),
                                   start=(k == 0), stop=(k == kk - 1))
                i.then_inc(unit_done, 1)

            def tokens_first(u, kk, lhs, width=COLS):
                banks_free(u)
                for s in range(2):
                    pe.wait_ge(slot_full[2 * u.r + s], u.full())
                    for a in range(2):
                        for k in range(kk):
                            i = mm(banks[2 * u.r + s][:, a * COLS:(a + 1) * COLS], lhs(k, a), slot(u, s, kk)[:, k, :],
                                   start=(k == 0), stop=(k == kk - 1))
                i.then_inc(unit_done, 1)

            def deep(u, kk, rhs, ready=None):
                banks_free(u)
                for s in range(2):
                    pe.wait_ge(slot_full[2 * u.r + s], u.full())
                for t in range(2):
                    for k in range(kk):
                        s, j = divmod(k, kk // 2)
                        if ready and t == 0:
                            ready(k)
                        i = mm(banks[2 * u.r][:, t * T:(t + 1) * T], slot(u, s, kk // 2)[:, j, t * P:(t + 1) * P], rhs(k),
                               start=(k == 0), stop=(k == kk - 1))
                i.then_inc(unit_done, 1)

            def norm(name):
                n = NORMS[name][0]
                for k in range(KD):
                    if k in (0, X_HEAD[name]):
                        pe.wait_ge(sq_ready, 2 * n + 1 + (k > 0))
                    i = mm(bank_sum[:, 0:T], ones[:, 0:P], sq[:, k, :], start=(k == 0), stop=(k == KD - 1))
                i.then_inc(sum_ready, 1)

            def h_of(name):
                n = H_BEFORE[name]
                return lambda k: pe.wait_ge(h_ready, KD * n + k + 1)

            def h(k):
                return hT[:, k, :]

            def mod_sums(u, parts, bank):
                for s in range(2):
                    for t in range(2):
                        i = mm(bank[:, 2 * s + t:2 * s + t + 1], parts[:, s, t * P:(t + 1) * P], ones[:, 0:1],
                               start=True, stop=True)
                i.then_inc(unit_done, 1)

            def mod_em():
                pe.wait_ge(x_ready, 1)
                for i in range(6):
                    u = Unit(base["mod_em"] + i)
                    banks_free(u)
                    pe.wait_ge(mod_dve, MOD_STEPS * (i + 1))
                    mod_sums(u, em_parts(i), banks[2 * u.r])

            def mod_ef(i):
                u = Unit(base["mod_ef"] + i)
                pe.wait_ge(mod_pool, 2 * (i + 1))
                pe.wait_ge(evac, base["mod_ef"] + max(i - 1, 0))
                mod_sums(u, ef_parts(i), ef_bank(i))

            def even_ffn():
                norm("ef")
                first = base["even_ffn"]
                ready = h_of("ef")

                def modulation(u, which, i, place):
                    banks_free(u)
                    pe.wait_ge(mod_dve, (i + (6 * which + 7)) * MOD_STEPS)
                    mod_sums(u, ffn_mod_parts(place), banks[2 * u.r])

                def hidden(k):
                    pe.wait_ge(evac, first + max(k // 2 * 2, 1))
                mod_in_ffn(pe, first, lambda u, i: wide(u, KD, h, ready if u.c == first else None), modulation,
                           lambda u, i: deep(u, KF, lambda k: act[:, k, :], hidden if i == 0 else None))

            def ffn(stage, name):
                norm(name)
                first, n = base[stage], SPLIT.index(stage)

                def three_passes(out, terms, blocks, ready=None):
                    for p, (w, x) in enumerate(terms):
                        for k in range(blocks):
                            if ready:
                                ready(p, k)
                            i = mm(out, w(k), x(k), start=(p == k == 0), stop=(p == 2 and k == blocks - 1))
                    return i

                def h_parts(p, k):
                    if p == 0:
                        pe.wait_ge(h_high, KD * n + k + 1)
                    if p == 2:
                        pe.wait_ge(h_low, KD * n + k + 1)

                def gate_up(u, i):
                    banks_free(u)
                    for s in range(2):
                        pe.wait_ge(w_low, slots_before(stage, i) + (s + 1))
                        high, low = gate_up_high(stage, u, s), slot(u, s, KD, rounded=True)
                        for t in range(2):
                            cols = slice(t * P, (t + 1) * P)
                            w_hi, w_lo = lambda k: high[:, k, cols], lambda k: low[:, k, cols]
                            x_hi, x_lo = lambda k: h_hi[:, k, :], lambda k: h_lo[:, k, :]
                            ins = three_passes(banks[2 * u.r + s][:, t * T:(t + 1) * T],
                                              ((w_hi, x_hi), (w_lo, x_hi), (w_hi, x_lo)), KD,
                                              h_parts if u.c == first and s == t == 0 else None)
                    ins.then_inc(unit_done, 1)

                def act_parts(p, k):
                    if p == 0:
                        pe.wait_ge(act_high, GU_UNITS * n + k // 2 + 1)
                    if p == 2:
                        pe.wait_ge(act_low, GU_UNITS * n + k // 2 + 1)

                def down(i):
                    u = Unit(first + GU_UNITS + i)
                    banks_free(u)
                    pe.wait_ge(w_low, slots_before(stage, GU_UNITS + i) + 2)
                    for t in range(2):
                        cols = slice(t * P, (t + 1) * P)
                        w_hi = lambda k: down_high(i, k // 11)[:, k % 11, cols]
                        w_lo = lambda k: slot(u, k // 11, 11, rounded=True)[:, k % 11, cols]
                        x_hi, x_lo = lambda k: act_hi[:, k, :], lambda k: act_lo[:, k, :]
                        ins = three_passes(banks[2 * u.r][:, t * T:(t + 1) * T],
                                          ((w_hi, x_hi), (w_lo, x_hi), (w_hi, x_lo)), KF,
                                          act_parts if i == t == 0 else None)
                    ins.then_inc(unit_done, 1)

                gate_up(Unit(first), 0)
                repeat(pe, first + 1, GU_UNITS - 1, lambda u, i: gate_up(u, i + 1))
                for i in range(DN_UNITS):
                    down(i)

            def attention(at, banks_ready):
                def scores(h):
                    g = at.first + h
                    if h >= 2:
                        pe.wait_ge(score_max, g - 1)
                    bank = banks[h % 2]
                    for a in range(2):
                        w = at.widths[a]
                        i = mm(bank[:, at.span(a)], at.q[at.part(h), h // 2, a * P:(a + 1) * P], at.k[at.part(h), h // 2, 0:w],
                               start=True, stop=False)
                        i = mm(bank[:, at.span(a)], *at.bias(h, a), start=False, stop=True)
                    i.then_inc(score_ready, 1)

                def turn(h):
                    g = at.first + h
                    pe.wait_ge(prob_ready, g + 1)
                    if h >= 2:
                        pe.wait_ge(prob_cp, g - 1)
                    bank = banks[2 + h % 2]
                    for a in range(2):
                        for b in range(at.widths[a] // P):
                            col = b * T + a * P - (P if b == 1 and at.widths[0] == P else 0)
                            i = nc.tensor.transpose(bank[:, col:col + P],
                                                    probs[:, h % 2, at.widths[0] * a + b * P:at.widths[0] * a + (b + 1) * P],
                                                    ident[:, :])
                    i.then_inc(prob_tr, 1)

                def outputs(h):
                    g = at.first + h
                    pe.wait_ge(prob_cp, g + 1)
                    if h >= 4 and h % 2 == 0:
                        pe.wait_ge(heads_read, g // 2 - 1)
                    bank = banks[4 + (h // 2) % 2]
                    late = P if at.widths[0] == P else 0
                    mm(bank[at.part(h), 0:T], at.v[:, 0, h * DH:(h + 1) * DH], probsT[:, h % 2, 0:T], start=True, stop=False)
                    mm(bank[at.part(h), late:T], at.v[:, 1, h * DH:(h + 1) * DH], probsT[:, h % 2, T:2 * T - late],
                       start=False, stop=True).then_inc(head_out, 1)

                banks_ready()
                for step in range(at.heads + 2):
                    if step < at.heads:
                        scores(step)
                    if 0 <= step - 1 < at.heads:
                        turn(step - 1)
                    if step >= 2:
                        outputs(step - 2)
                    if at is FOX and has("mod_ef") and step in EF_AT:
                        mod_ef(EF_AT[step])

            def even_mixer():
                norm("em")
                first = base["even_in"]
                ready = h_of("em")
                u = Unit(first)
                banks_free(u)
                for s, n in ((0, 8), (1, 16)):
                    pe.wait_ge(slot_full[2 * u.r + s], u.full())
                    for k in range(KD):
                        if s == 0:
                            ready(k)
                        i = mm(banks[2 * u.r + s][0:n, 0:T], slot(u, s, KD)[:, k, 0:n], h(k), start=(k == 0), stop=(k == KD - 1))
                i.then_inc(unit_done, 1)
                by_token = lambda k, a: hT[:, k, a * P:(a + 1) * P]
                wide(Unit(first + 1), KD, h)
                tokens_first(Unit(first + 2), KD, by_token)
                pe.wait_ge(evac, first + 1)
                pe.wait_ge(cols_in, 16 * (len(COL_LOADS) + 3))
                for j in range(2):
                    i = mm(bank_x[:, j * T:(j + 1) * T], gla_w2[:, j * P:(j + 1) * P], soft[0:16, 2, :], start=True, stop=True)
                i.then_inc(decay_ps, 1)
                wide(Unit(first + 3), KD, h)
                wide(Unit(first + 4), KD, h)
                tokens_first(Unit(first + 5), KD, by_token)
                wide(Unit(first + 6), KD, h)

                pe.wait_ge(evac, first + 7)
                pe.wait_ge(query_ready, 1)
                for i in range(NB):
                    pe.wait_ge(key_ready, i + 1)
                    kd = gla_kd[:, 2 * (i % 3):2 * (i % 3) + 2, :]
                    for hd in range(4):
                        part = slice(DH * (hd % 2), DH * (hd % 2) + DH)
                        q = gla_qd[part, hd // 2, i * GB:(i + 1) * GB]
                        for s in range(2 if i >= NB // 2 else 1):
                            col = i * GB if s == 0 else T + i * GB - P
                            ins = mm(banks[hd][:, col:col + GB], kd[part, hd // 2, s * P:(s + 1) * P], q, start=True, stop=True)
                    ins.then_inc(key_used, 1)
                for hd in range(4):
                    pe.wait_ge(gla_masked, hd + 1)
                    bank, c = banks[4 + hd // 2], (hd % 2) * T
                    mm(bank[:, c:c + T], gla_v[:, 0, hd * P:(hd + 1) * P], gla_a[:, hd, 0:T], start=True, stop=False)
                    mm(bank[:, c + P:c + T], gla_v[:, 1, hd * P:(hd + 1) * P], gla_a[:, hd, T:T + P],
                       start=False, stop=True).then_inc(gla_out, 1)
                for hd in range(4):
                    pe.wait_ge(gla_sq, hd // 2 + 1)
                    i = mm(banks[6 + hd // 2][:, (hd % 2) * T:(hd % 2 + 1) * T], ones[:, 0:P], gla_osq[:, hd, :],
                           start=True, stop=True)
                i.then_inc(gla_sum, 1)
                attention(FOX, lambda: pe.wait_ge(gla_done, 1))
                pe.wait_ge(heads_read, n_fox // 2)

            def s5_prep():
                pe.wait_ge(s5_rows, 1)
                for n, row in enumerate((6, 5, 12, 13)):
                    i = nc.tensor.transpose(bank_x[:, n * NS:(n + 1) * NS], prm(row), ident[0:NS, 0:NS])
                i.then_inc(s5_tr, 1)

            def s5_in():
                norm("om")
                first = base["s5_in"]
                wide(Unit(first), KD, h, h_of("om"))
                wide(Unit(first + 1), KD, h)
                pe.wait_ge(evac, first + 2)
                pe.wait_ge(b_exp, 1)
                for n in range(2):
                    for m in range(8):
                        i = nc.tensor.transpose(banks[2 * n + m // 4][:, (m % 4) * P:(m % 4 + 1) * P],
                                                flat2(b_wide[n])[:, m * P:(m + 1) * P], ident[:, :])
                i.then_inc(bc_tr, 1)
                pe.wait_ge(c_exp, 1)
                pe.wait_ge(bc_cp, 1)
                for n in range(2):
                    for m in range(8):
                        i = nc.tensor.transpose(banks[2 * n + m // 4][:, (m % 4) * P:(m % 4 + 1) * P],
                                                c_wide[n][:, m, :, :].rearrange("p j q -> p (j q)"), ident[:, :])
                i.then_inc(bc_tr, 1)
                pe.wait_ge(bc_cp, 2)
                for i in range(NS + 2):
                    if i < NS:
                        m, part = i // 4, slice(32 * (i % 4), 32 * (i % 4) + 32)
                        if i >= 3:
                            pe.wait_ge(bu_turned, i - 2)
                        for n in range(2):
                            ins = mm(banks[i % 3][:, n * T:(n + 1) * T], bT[n][part, m, :], act[part, m, :], start=True, stop=True)
                        ins.then_inc(bu_ready, 1)
                    if i >= 2:
                        j = i - 2
                        m, part = j // 4, slice(32 * (j % 4), 32 * (j % 4) + 32)
                        pe.wait_ge(w_ready, j + 1)
                        if m >= 3 and j % 4 == 0:
                            pe.wait_ge(y_read, m - 2)
                        for n in range(2):
                            ins = mm(banks[3 + m % 3][part, 0:T], cT[n][:, m, part], s5_u1[j % 2][:, n, :],
                                     start=(n == 0), stop=(n == 1))
                        ins.then_inc(w_used, 1)
                pe.wait_ge(y_read, 8)

            def moe():
                norm("of")
                ready = h_of("of")
                first = base["moe"]
                pe.wait_ge(cols_in, 16 * (len(COL_LOADS) + 3))
                for a in range(2):
                    for k in range(KD):
                        if a == 0:
                            ready(k)
                        i = mm(bank_x[:, a * 8:(a + 1) * 8], hT[:, k, a * P:(a + 1) * P], router[:, k, :],
                               start=(k == 0), stop=(k == KD - 1))
                i.then_inc(logit_ready, 1)
                pe.wait_ge(evac, first)
                for b in range(4):
                    a, half = divmod(b, 2)
                    for j in range(4):
                        i = nc.tensor.transpose(banks[b][:, j * P:(j + 1) * P], hT[:, 4 * half + j, a * P:(a + 1) * P], ident[:, :])
                    i.then_inc(tok_tr, 1)
                pe.wait_ge(mask_ready, 1)
                chosen = [route[:, CHOSEN + a, 0:8] for a in range(2)]
                mm(bank_sum[:, 0:8], upper[:, 0, :], chosen[0], start=True, stop=True)
                mm(bank_sum[:, 8:16], ones[:, 0:P], chosen[0], start=True, stop=False)
                mm(bank_sum[:, 8:16], upper[:, 0, :], chosen[1], start=False, stop=True)
                mm(bank_sum[:, 16:24], ones[:, 0:P], chosen[0], start=True, stop=False)
                mm(bank_sum[:, 16:24], ones[:, 0:P], chosen[1], start=False, stop=True).then_inc(pos_ready, 1)
                pe.wait_ge(tok_cp, 4)
                pe.wait_ge(routed, 1)
                two = (bank_sum, bank_x)

                def units_256(e):
                    def gate_up(u, i):
                        pe.wait_ge(gather_cp, e * 4 + 4)
                        wide(u, KD, lambda k: xg[:, k, 0:T])
                    repeat(pe, first, GU_UNITS, gate_up, outer=e * 5)
                    pe.wait_ge(evac, Unit(first, e * 5).at(GU_UNITS))
                    for i in range(DN_UNITS):
                        u = Unit(first + GU_UNITS + i, e * 5)
                        banks_free(u)
                        for s in range(2):
                            pe.wait_ge(slot_full[2 * u.r + s], u.full())
                        for a in range(2):
                            for k in range(KF):
                                s, j = divmod(k, KF // 2)
                                ins = mm(banks[2 * u.r][:, a * COLS:(a + 1) * COLS], act[:, k, a * P:(a + 1) * P],
                                         slot(u, s, KF // 2)[:, j, :], start=(k == 0), stop=(k == KF - 1))
                        ins.then_inc(unit_done, 1)

                def gate_up_128(u, i, e):
                    banks_free(u)
                    pe.wait_ge(hid_low, e * GU_UNITS + (i + 1))
                    for s in range(2):
                        pe.wait_ge(w_low, slots_before("moe", e * 15 + i) + (s + 1))
                        high, low = gate_up_high("moe", u, s), slot(u, s, KD, rounded=True)
                        for p, (x, w) in enumerate(((HIGH, high), (HIGH, low), (LOW, high))):
                            for k in range(KD):
                                ins = mm(banks[2 * u.r + s][:, 0:COLS], xg_r[:, k, x], w[:, k, :],
                                         start=(p == k == 0), stop=(p == 2 and k == KD - 1))
                    ins.then_inc(unit_done, 1)

                def turn_hidden(u):
                    pe.wait_ge(evac, u.at(1))
                    for t in range(2):
                        ins = nc.tensor.transpose(banks[2 * u.r][:, T + t * P:T + (t + 1) * P],
                                                  silu_g[:, u.r, T + t * P:T + (t + 1) * P], ident[:, :])
                    ins.then_inc(hid_turned, 1)

                def units_128(e):
                    pe.wait_ge(xg_low, e * 4 + 4)

                    def step(u, i):
                        gate_up_128(u, i, e)
                        turn_hidden(Unit(u.c - 1, u.v))
                    gate_up_128(Unit(first, e * 5), 0, e)
                    repeat(pe, first + 1, GU_UNITS - 1, lambda u, i: step(u, i + 1), outer=e * 5)
                    turn_hidden(Unit(first + GU_UNITS - 1, e * 5))
                    for i in range(DN_UNITS):
                        u = Unit(first + GU_UNITS + i, e * 5)
                        banks_free(u)
                        for k in range(KF):
                            if k % 11 == 0:
                                pe.wait_ge(w_low, slots_before("moe", e * 15 + (GU_UNITS + i)) + (k // 11 + 1))
                            if i == 0 and k % 2 == 0:
                                pe.wait_ge(hid_low, e * GU_UNITS + (k // 2 + 4))
                            high = down_high(i, k // 11, "moe")[:, k % 11, :]
                            low = slot(u, k // 11, 11, rounded=True)[:, k % 11, :]
                            for p, (x, w) in enumerate(((HIGH, high), (HIGH, low), (LOW, high))):
                                ins = mm(banks[2 * u.r][:, 0:COLS], act_r[:, k, x], w,
                                         start=(p == k == 0), stop=(p == 2 and k == KF - 1))
                        ins.then_inc(unit_done, 1)

                def expert(e, n):
                    if n > P:
                        pe.sem_inc(hid_turned, GU_UNITS)
                    pe.wait_ge(pick_ready, e + 1)
                    pe.wait_ge(scatter_read, e * 4 + 1)
                    for s in range(n // P):
                        for a in range(2):
                            i = nc.tensor.transpose(bank_x[:, s * T + a * P:s * T + (a + 1) * P],
                                                    pick_w[:, a, s * P:(s + 1) * P], ident[:, :])
                    i.then_inc(pick_tr, 1)
                    for j in range(4):
                        if j == 1:
                            pe.wait_ge(pick_cp, e + 1)
                        if j >= 2:
                            pe.wait_ge(gather_cp if n > P else xg_low, e * 4 + (j - 1))
                        for t in range(2):
                            for a in range(2):
                                k = 2 * j + t
                                i = mm(two[j % 2][:, t * n:(t + 1) * n], h_tok[:, a, k * P:(k + 1) * P], pick[:, a, 0:n],
                                       start=(a == 0), stop=(a == 1))
                        i.then_inc(gathered, 1)

                    (units_256 if n > P else units_128)(e)
                    pe.wait_ge(evac, Unit(first, e * 5).at(GU_UNITS + DN_UNITS))
                    for j in range(4):
                        if j >= 2:
                            pe.wait_ge(scatter_read, e * 4 + j)
                        for t in range(2):
                            m = 2 * j + t
                            for s in range(n // P):
                                ins = mm(two[j % 2][:, t * T:(t + 1) * T], yg[:, s, m * P:(m + 1) * P], pick_t[:, s, :],
                                         start=(s == 0), stop=(s == n // P - 1))
                        ins.then_inc(scattered, 1)

                by_count(pe, expert)

            def ssd():
                norm("mix_0")
                first = base["ssd_in"]
                ready = h_of("mix_0")
                u = Unit(first)
                banks_free(u)
                for s in range(2):
                    pe.wait_ge(slot_full[2 * u.r + s], u.full())
                    for k in range(KD):
                        if s == 0:
                            ready(k)
                        i = mm(banks[2 * u.r][NH * s:NH * (s + 1), 0:T], slot(u, s, KD)[:, k, 0:NH], h(k),
                               start=(k == 0), stop=(k == KD - 1))
                i.then_inc(unit_done, 1)
                repeat(pe, first + 1, 16, lambda u, i: wide(u, KD, h))
                pe.wait_ge(dt_ready, 1)
                for n, rows in enumerate((run_rows, dt_rows)):
                    for s in range(2):
                        nc.tensor.transpose(bank_x[:, n * P + s * 64:n * P + s * 64 + 64], rows[0:64, 0, s * P:(s + 1) * P],
                                            ident[0:64, 0:64])
                nc.tensor.transpose(bank_x[:, T:T + 16], d_rows[:, 0:P], ident[0:16, 0:16]).then_inc(dt_tr, 1)
                pe.wait_ge(xs_ready, 12)
                pe.wait_ge(dt_cols, 1)
                row_banks = (0, 1, 2, 5)

                def pair(g, n):
                    if n == 0:
                        pe.wait_ge(weights_f, g + 1)
                        pe.wait_ge(weights_b, g + 1)
                    if g >= 1:
                        pe.wait_ge(pair_read, 2 * g - 1 + n)
                    for j in range(2):
                        hd = 2 * n + j
                        o = banks[3 + n][64 * j:64 * j + 64, :]
                        f, b = (ssd_seg[g % 2][d][:, hd * 3 * P:(hd + 1) * 3 * P] for d in range(2))
                        xf, xb = (ssd_x[g % 2][d][:, :, hd * 64:(hd + 1) * 64] for d in range(2))
                        mm(o[:, 0:T], xf[:, 0, :], f[:, 0:T], start=True, stop=False)
                        mm(o[:, P:T], xf[:, 1, :], f[:, T:3 * P], start=False, stop=False)
                        mm(o[:, 0:P], xb[:, 0, :], b[:, 0:P], start=False, stop=False)
                        i = mm(o[:, 0:T], xb[:, 1, :], b[:, P:3 * P], start=False, stop=True)
                    i.then_inc(pair_ready, 1)

                for g in range(9):
                    if g < 8:
                        if g >= 1:
                            pe.wait_ge(xdt_ready, g)
                        for s in range(2):
                            for j in range(2):
                                i = nc.tensor.transpose(bank_x[:, s * T + j * P:s * T + (j + 1) * P],
                                                        arena[:, (2 * g + j) * T + s * P:(2 * g + j) * T + (s + 1) * P], ident[:, :])
                        i.then_inc(xs_tr, 1)
                        bf, cf, bb, cb = (arena[:, (16 + 8 * n + g) * T:(17 + 8 * n + g) * T] for n in range(4))
                        if g >= 1:
                            pe.wait_ge(cb_masked, 2 * g)
                        mm(bank_sum[:, 0:T], bf[:, 0:P], cf, start=True, stop=True)
                        mm(bank_sum[:, T:3 * P], bf[:, P:T], cf[:, P:T], start=True, stop=True).then_inc(cb_ready, 1)
                        pe.wait_ge(cb_masked, 2 * g + 1)
                        mm(bank_sum[:, 0:P], bb[:, 0:P], cb[:, 0:P], start=True, stop=True)
                        mm(bank_sum[:, P:3 * P], bb[:, P:T], cb, start=True, stop=True).then_inc(cb_ready, 1)
                        for d in range(2):
                            for n in range(2):
                                q = 2 * d + n
                                if g >= 1:
                                    pe.wait_ge(rows_read, 4 * (g - 1) + q + 1)
                                for j in range(2):
                                    r = 32 * d + 4 * g + 2 * n + j
                                    i = mm(banks[row_banks[q]][:, j * T:(j + 1) * T], ident[0:64, r:r + 1].to_broadcast([64, P]),
                                           run_rows[0:64, 0, :], start=True, stop=True)
                                i.then_inc(rows_ready, 1)
                    if g >= 1:
                        for n in range(2):
                            pair(g - 1, n)
                for k in range(16):
                    if k % 8 == 0:
                        pe.wait_ge(y_sq, k // 8 + 1)
                    i = mm(bank_sum[:, 0:T], ones[:, 0:P], sq[:, k, :] if k < 8 else hT[:, k - 8, :], start=(k == 0), stop=(k == 15))
                i.then_inc(y_sum, 1)

            def na():
                norm("mix_1")
                first = base["na_in"]

                def head_sums(n):
                    pe.wait_ge(qk_sq, n + 1)
                    if n >= 1:
                        pe.wait_ge(qk_std, n)
                    for j in range(4):
                        i = mm(banks[6 + j // 2][:, (j % 2) * T:(j % 2 + 1) * T], halves[:, :], sq[:, 4 * (n % 2) + j, :],
                               start=True, stop=True)
                    i.then_inc(qk_sum, 1)
                wide(Unit(first), KD, h, h_of("mix_1"))
                for c in range(1, 4):
                    wide(Unit(first + c), KD, h)
                    head_sums(c - 1)
                tokens_first(Unit(first + 4), KD, lambda k, a: hT[:, k, a * P:(a + 1) * P])
                head_sums(3)
                tokens_first(Unit(first + 5), KD, lambda k, a: hT[:, k, a * P:(a + 1) * P])

                def banks_ready():
                    pe.wait_ge(evac, first + 6)
                    pe.wait_ge(qk_ready, 4)
                    pe.wait_ge(rpb_in, 16 * 12)
                attention(NA, banks_ready)

            def out_product(stage, ready):
                for i in range(STAGE_UNITS[stage]):
                    wide(Unit(base[stage] + i), KD, lambda k: act[:, k, :], ready if i == 0 else None)
                    if stage == "even_out" and i == 0 and has("s5_prep"):
                        s5_prep()

            def ple(stage):
                i = int(stage[4])
                norm(stage)
                ready = h_of(stage)
                for c in range(2):
                    wide(Unit(base[stage] + c), KD, h, ready if c == 0 else None)
                pe.wait_ge(p_in, 16 * (i + 1))
                for f in range(2):
                    for a in range(2):
                        ins = nc.tensor.transpose(bank_x[:, f * T + a * P:f * T + (a + 1) * P],
                                                  p_tok[:, a, f * P:(f + 1) * P], ident[:, :])
                ins.then_inc(p_tr, 1)
                pe.wait_ge(p_cp, i + 1)
                for c in range(2, 4):
                    wide(Unit(base[stage] + c), 2, lambda k: pT[:, k, :])
                pe.wait_ge(post_sq, i + 1)
                for k in range(KD):
                    ins = mm(bank_sum[:, 0:T], ones[:, 0:P], sq[:, k, :], start=(k == 0), stop=(k == KD - 1))
                ins.then_inc(post_sum, 1)

            for stage in stages:
                if stage == "mod_em":
                    mod_em()
                if stage == "even_in":
                    even_mixer()
                if stage == "even_out":
                    out_product(stage, None)
                if stage == "s5_in":
                    s5_in()
                if stage == "s5_glu":
                    for i in range(2):
                        wide(Unit(base[stage] + i), KD, lambda k: act[:, 8 + k, :],
                             (lambda k: pe.wait_ge(y_gelu, k + 1)) if i == 0 else None)
                if stage == "s5_out":
                    out_product(stage, lambda k: pe.wait_ge(evac, base["s5_glu"] + k // 4 + 1))
                if stage == "moe":
                    moe()
                if stage == "ssd_in":
                    ssd()
                if stage == "ssd_out":
                    for i in range(4):
                        deep(Unit(base[stage] + i), 16, lambda k: arena[:, k * T:(k + 1) * T],
                             (lambda k: pe.wait_ge(y_normed, k + 1)) if i == 0 else None)
                if stage == "na_in":
                    na()
                if stage == "na_out":
                    pe.wait_ge(heads_read, n_fox // 2 + 8)
                    out_product(stage, None)
                if stage == "even_ffn":
                    even_ffn()
                if stage[:5] in ("ffn1_", "ffn2_"):
                    ffn(stage, stage)
                if stage == "final":
                    norm("final")
                if stage[:4] == "ple_":
                    ple(stage)

            pe.wait_ge(*X_AT["end"])
            for b in range(4):
                a, half = divmod(b, 2)
                for j in range(4):
                    k = 4 * half + j
                    i = nc.tensor.transpose(banks[b][:, j * P:(j + 1) * P], xT[:, k, a * P:(a + 1) * P], ident[:, :])
                i.then_inc(out_tr, 1)

        @block.scalar
        def _(se):
            activation = nc.scalar.activation
            tally = Tally(a_chain)
            loads = vec_loads[1::2]
            for dst, src in loads[:6]:
                nc.scalar.dma_start(dst, src).then_inc(vec_in, 16)
            se.wait_ge(c_in, 16)
            activation(csil[:, :], c_raw_cols[:, :], ACT.Silu).then_inc(csil_ready, 1)
            for dst, src in loads[6:]:
                nc.scalar.dma_start(dst, src).then_inc(vec_in, 16)

            def norm(name, meanwhile=None):
                n, _, shift = NORMS[name]
                updates, value = X_AT[name]
                head = X_HEAD[name]
                if updates is not x_ready:
                    value -= 1
                se.wait_ge(updates, value)
                activation(sq[:, 0:head, :], xT[:, 0:head, :], ACT.Square).then_inc(sq_ready, 1)
                se.wait_ge(*X_AT[name])
                activation(sq[:, head:, :], xT[:, head:, :], ACT.Square).then_inc(sq_ready, 1)
                if meanwhile:
                    meanwhile()
                se.wait_ge(sum_ready, n + 1)
                activation(std[:, 0:T], bank_sum[:, 0:T], ACT.Sqrt, bias=small[:, 0:1], scale=1.0 / D).then_inc(std_ready, 1)
                if shift:
                    for k in range(KD):
                        se.wait_ge(scaled, KD * n + k + 1)
                        activation(hT[:, k, :], hT[:, k, :], ACT.Identity, bias=shift(k)).then_inc(h_ready, 1)

            def even_ffn():
                norm("ef")
                mod_in_ffn(se, base["even_ffn"], lambda u, i: silu(u), lambda *a: None, lambda u, i: None)

            def high_part(u, s, kk, dst):
                se.wait_ge(slot_full[2 * u.r + s], u.full())
                activation(dst, slot(u, s, kk), ACT.Copy).then_inc(w_high, 1)

            def ffn(stage, name):
                first = base[stage]

                def gate_up(u):
                    for s in range(2):
                        high_part(u, s, KD, gate_up_high(stage, u, s))

                def down(i):
                    u = Unit(first + GU_UNITS + i)
                    se.wait_ge(unit_done, u.at(-1))
                    for s in range(2):
                        high_part(u, s, 11, down_high(i, s))

                def hidden(u, i):
                    se.wait_ge(evac, u.at(1))
                    pair = act[:, 2 * i:2 * i + 2, :] if isinstance(i, int) else act[:, bass.ds(i * 2, 2), :]
                    high = act_hi[:, 2 * i:2 * i + 2, :] if isinstance(i, int) else act_hi[:, bass.ds(i * 2, 2), :]
                    activation(high, pair, ACT.Copy).then_inc(act_high, 1)

                def step(u, i):
                    if u.c == first + GU_UNITS - 1:
                        down(0)
                    else:
                        se.wait_ge(unit_done, u.at(2 - SETS))
                        gate_up(next_unit(u))
                    silu(u)
                    if u.c > first:
                        hidden(Unit(u.c - 1, u.v), i - 1)

                norm(name, meanwhile=lambda: gate_up(Unit(first)))
                for k in range(KD):
                    se.wait_ge(h_ready, KD * H_BEFORE[name] + k + 1)
                    activation(h_hi[:, k, :], hT[:, k, :], ACT.Copy).then_inc(h_high, 1)
                step(Unit(first), 0)
                repeat(se, first + 1, GU_UNITS - 1, lambda u, i: step(u, i + 1))
                hidden(Unit(first + GU_UNITS - 1), GU_UNITS - 1)
                for i in range(1, DN_UNITS):
                    down(i)

            def silu(u):
                se.wait_ge(unit_done, u.at(1))
                if u.c >= SETS or not isinstance(u.v, int):
                    se.wait_ge(evac, u.at(1 - SETS))
                activation(silu_g[:, u.r, :], banks[2 * u.r][:, :], ACT.Silu).then_inc(silu_ready, 1)

            def store(stage, i, dst, func=ACT.Copy, scale=1.0):
                u = Unit(base[stage] + i)
                se.wait_ge(unit_done, u.at(1))
                for s in range(2):
                    ins = activation(dst(s), banks[2 * u.r + s][:, :], func, scale=scale)
                ins.then_inc(evac, 1)

            def flat(t):
                return t.rearrange("p k t -> p (k t)")

            def by_half(v, s):
                return v[:, :, s * COLS:(s + 1) * COLS]

            def store_tokens(stage, i, v, col0=0):
                u = Unit(base[stage] + i)
                se.wait_ge(unit_done, u.at(1))
                for s in range(2):
                    ins = activation(v[:, :, col0 + s * COLS:col0 + (s + 1) * COLS],
                                     banks[2 * u.r + s][:, :].rearrange("p (a m) -> p a m", a=2), ACT.Copy)
                ins.then_inc(evac, 1)

            def softplus_of_minus_abs(x, p):
                tally.up(activation(x[1], x[0], ACT.Abs))
                tally.wait(se)
                tally.up(activation(x[1], x[1], ACT.Exp, scale=-1.0))
                tally.wait(se)
                activation(x[1], x[1], ACT.Ln, bias=ones[0:p, 0:1]).then_inc(soft_ready, 1)

            def attention(at):
                def exps(h):
                    g = at.first + h
                    se.wait_ge(score_max, g + 1)
                    for a in range(2):
                        ins = activation(probs[:, h % 2, at.span(a)], probs[:, h % 2, at.span(a)], ACT.Exp,
                                         bias=row_max[:, h % 2, a:a + 1], accum_out=row_sum[:, h % 2, a:a + 1])
                    ins.then_inc(prob_exp, 1)

                def copy(h):
                    g = at.first + h
                    se.wait_ge(prob_tr, g + 1)
                    if h >= 2:
                        se.wait_ge(head_out, g - 1)
                    n = sum(at.widths)
                    activation(probsT[:, h % 2, 0:n], banks[2 + h % 2][:, 0:n], ACT.Copy).then_inc(prob_cp, 1)

                def read(j):
                    se.wait_ge(head_out, at.first + 2 * j + 2)
                    activation(at.out(j), banks[4 + j % 2][:, 0:T], ACT.Copy).then_inc(heads_read, 1)

                for step in range(at.heads + 3):
                    if step < at.heads:
                        exps(step)
                    if 0 <= step - 1 < at.heads:
                        copy(step - 1)
                    if step >= 4 and step % 2 == 0:
                        read(step // 2 - 2)

            def even_mixer():
                norm("em")
                st = "even_in"
                se.wait_ge(cols_in, 16 * (len(COL_LOADS) + 3))
                u = Unit(base[st])
                se.wait_ge(unit_done, u.at(1))
                activation(gate_in[0:8, 2, :], banks[2 * u.r][0:8, 0:T], ACT.Identity, bias=small[0:8, FB_COL:FB_COL + 1])\
                    .then_inc(gate_x, 1)
                activation(soft[0:16, 2, :], banks[2 * u.r + 1][0:16, 0:T], ACT.Copy).then_inc(evac, 1)
                se.wait_ge(gate_x, 1)
                softplus_of_minus_abs((gate_in[0:8, 2, :], gate_low[0:8, 0, :]), 8)
                store(st, 1, lambda s: flat(gla_q if s == 0 else gla_k))
                store_tokens(st, 2, gla_v)
                se.wait_ge(decay_ps, 1)
                for j in range(2):
                    tally.up(activation(gate_in[:, j, :], bank_x[:, j * T:(j + 1) * T], ACT.Identity, bias=vcol("e_gla_b2", j)))
                tally.wait(se)
                se.wait_ge(evac, base[st] + 3)
                nc.scalar.activation(soft[:, 0:2, :], gate_in[:, 0:2, :], ACT.Abs).then_inc(decay_x, 1)
                se.wait_ge(decay_x, 1)
                tally.up(activation(soft[:, 0:2, :], soft[:, 0:2, :], ACT.Exp, scale=-1.0))
                tally.wait(se)
                activation(soft[:, 0:2, :], soft[:, 0:2, :], ACT.Ln, bias=ones[:, 0:1]).then_inc(soft_ready, 1)
                store(st, 3, lambda s: flat(fox_q[:, 2 * s:2 * s + 2, :]), scale=DH ** -0.5)
                store(st, 4, lambda s: flat(fox_k[:, 2 * s:2 * s + 2, :]))
                se.wait_ge(query_raw, 1)
                activation(gla_qd[:, :, :], gla_qd[:, :, :], ACT.Exp, scale=1.0 / 16.0).then_inc(query_exp, 1)

                def key(i):
                    se.wait_ge(key_raw, i + 1)
                    w = P if i < NB // 2 else T
                    kd = gla_kd[:, 2 * (i % 3):2 * (i % 3) + 2, 0:w]
                    activation(kd, kd, ACT.Exp, scale=-1.0 / 16.0).then_inc(key_exp, 1)
                for i in range(3):
                    key(i)
                store_tokens(st, 5, fox_v)
                store(st, 6, lambda s: flat(gla_g[:, 2 * s:2 * s + 2, :]), ACT.Silu)
                for i in range(3, NB):
                    key(i)
                for j in range(2):
                    se.wait_ge(gla_out, 2 * j + 2)
                    activation(flat(gla_osq[:, 2 * j:2 * j + 2, :]), banks[4 + j][:, :], ACT.Square).then_inc(gla_sq, 1)
                se.wait_ge(gla_sum, 1)
                for j in range(2):
                    ins = activation(std[:, j * 2 * T:(j + 1) * 2 * T], banks[6 + j][:, :], ACT.Sqrt, bias=small[:, 0:1], scale=1.0 / P)
                ins.then_inc(gla_std, 1)
                attention(FOX)

            def s5_prep():
                se.wait_ge(prm_in, 48)
                activation(prm(3, 2), prm(2, 2), ACT.Exp).then_inc(s5_dt, 1)
                se.wait_ge(s5_expo, 1)
                activation(prm(6), prm(7), ACT.Exp).then_inc(s5_mag, 1)
                se.wait_ge(s5_red, 1)
                activation(prm(8), prm(5), ACT.Sin)
                activation(prm(9), prm(5), ACT.Sin, scale=0.5).then_inc(s5_sin, 1)

            def s5_tables():
                for c in range(NS // 4):
                    se.wait_ge(range_ready, 2 * c + 2)
                    r = s5_cos[:, 4 * c:4 * c + 4, :]
                    tally.up(activation(s5_sin_t[:, 4 * c:4 * c + 4, :], r, ACT.Sin))
                    tally.wait(se)
                    activation(r, r, ACT.Sin, scale=0.5).then_inc(sin_ready, 1)

            def s5_in():
                se.wait_ge(*X_AT["om"])
                for n, name in enumerate(("o_b_re", "o_b_im")):
                    nc.scalar.dma_start(b_raw[n], A[name][0].rearrange("(i g) q k -> (g q) i k", g=2)).then_inc(raw_in, 16)
                for n, name in enumerate(("o_c_re", "o_c_im")):
                    nc.scalar.dma_start(c_raw[n], A[name][0].rearrange("(m g) k q -> (g k) m q", g=8)).then_inc(raw_in, 16)
                norm("om")
                for i in range(2):
                    store("s5_in", i, lambda s: flat(act[:, 4 * i + 2 * s:4 * i + 2 * s + 2, :]))
                for step, dst in enumerate((bT, cT)):
                    se.wait_ge(bc_tr, step + 1)
                    for n in range(2):
                        for half in range(2):
                            ins = activation(dst[n][:, 4 * half:4 * half + 4, :].rearrange("p m s -> p (m s)"),
                                             banks[2 * n + half][:, :], ACT.Copy)
                    ins.then_inc(bc_cp, 1)
                for m in range(8):
                    se.wait_ge(y_read, m + 1)
                    activation(act[:, 8 + m, :], act[:, 8 + m, :], ACT.Gelu_apprx_tanh).then_inc(y_gelu, 1)

            def s5_glu():
                for i in range(2):
                    u = Unit(base["s5_glu"] + i)
                    se.wait_ge(unit_done, u.at(1))
                    for s in range(2):
                        ins = activation(arena[:, (4 * i + 2 * s) * T:(4 * i + 2 * s + 2) * T], banks[2 * u.r + s][:, :], ACT.Sigmoid)
                    ins.then_inc(glu_sig, 1)

            def moe():
                norm("of")
                first = base["moe"]
                for b in range(4):
                    a, half = divmod(b, 2)
                    se.wait_ge(tok_tr, b + 1)
                    activation(h_tok[:, a, half * 512:half * 512 + 512], banks[b][:, :], ACT.Copy).then_inc(tok_cp, 1)
                se.wait_ge(gap_ready, 1)
                activation(route[:, MISC:MISC + 2, 1:2], route[:, MISC:MISC + 2, 0:1], ACT.Exp).then_inc(gap_exp, 1)
                se.wait_ge(routed, 1)

                def expert(e, n):
                    split = n == P
                    if split:
                        se.wait_ge(unit_done, Unit(first, e * 5).at(0))
                        gate_up_high_parts(Unit(first, e * 5))
                    else:
                        se.sem_inc(w_high, 2 * (GU_UNITS + DN_UNITS))
                        se.sem_inc(hid_high, GU_UNITS)
                    se.wait_ge(pick_tr, e + 1)
                    activation(pick_t[:, 0:n // P, :], bank_x[:, 0:2 * n].rearrange("p (s t) -> p s t", t=T), ACT.Copy).then_inc(pick_cp, 1)
                    for j in range(4):
                        se.wait_ge(gathered, e * 4 + (j + 1))
                        activation((xg_r if split else xg)[:, 2 * j:2 * j + 2, 0:n],
                                   (bank_sum, bank_x)[j % 2][:, 0:2 * n].rearrange("p (k t) -> p k t", k=2), ACT.Copy).then_inc(gather_cp, 1)

                    def silu_units(u, i):
                        se.wait_ge(unit_done, u.at(1))
                        se.wait_ge(evac, u.at(1 - SETS))
                        activation(silu_g[:, u.r, 0:2 * n if n > P else COLS], banks[2 * u.r][:, 0:2 * n if n > P else COLS],
                                   ACT.Silu).then_inc(silu_ready, 1)

                    def step(u, i):
                        if isinstance(i, int) and i == GU_UNITS - 1:
                            down_high_parts(0, e)
                        else:
                            se.wait_ge(unit_done, u.at(2 - SETS))
                            gate_up_high_parts(next_unit(u))
                        silu_units(u, i)
                        if not isinstance(i, int) or i > 0:
                            hidden_high(Unit(u.c - 1, u.v), i - 1, e)
                    if split:
                        step(Unit(first, e * 5), 0)
                        repeat(se, first + 1, GU_UNITS - 1, lambda u, i: step(u, i + 1), outer=e * 5)
                        hidden_high(Unit(first + GU_UNITS - 1, e * 5), GU_UNITS - 1, e)
                    else:
                        repeat(se, first, GU_UNITS, silu_units, outer=e * 5)
                    for i in range(DN_UNITS):
                        if split and i + 1 < DN_UNITS:
                            down_high_parts(i + 1, e)
                        u = Unit(first + GU_UNITS + i, e * 5)
                        se.wait_ge(unit_done, u.at(1))
                        activation(yg[:, 0:n // P, i * COLS:(i + 1) * COLS],
                                   banks[2 * u.r][:, 0:2 * n].rearrange("p (s m) -> p s m", m=COLS), ACT.Copy).then_inc(evac, 1)

                def gate_up_high_parts(u):
                    for s in range(2):
                        high_part(u, s, KD, gate_up_high("moe", u, s))

                def down_high_parts(i, e):
                    u = Unit(first + GU_UNITS + i, e * 5)
                    se.wait_ge(unit_done, u.at(-1))
                    for s in range(2):
                        high_part(u, s, 11, down_high(i, s, "moe"))

                def hidden_high(u, i, e):
                    se.wait_ge(hid_turned, e * GU_UNITS + (i + 1))
                    dst = act_r[:, 2 * i:2 * i + 2, HIGH] if isinstance(i, int) else act_r[:, bass.ds(i * 2, 2), HIGH]
                    activation(dst, banks[2 * u.r][:, HIDDEN].rearrange("p (k t) -> p k t", k=2), ACT.Copy).then_inc(hid_high, 1)
                by_count(se, expert)

            def ssd():
                norm("mix_0")
                first = base["ssd_in"]
                se.wait_ge(cols_in, 16 * (len(COL_LOADS) + 3))
                activation(small[0:64, 8:9], small[0:64, ALOG_COL:ALOG_COL + 1], ACT.Exp).then_inc(a_exp, 1)
                for g in range(2):
                    ins = activation(d_rows[:, 64 * g:64 * g + 64], d_rows[:, P + g:P + g + 1].to_broadcast([16, 64]), ACT.Copy)
                ins.then_inc(a_exp, 1)
                u = Unit(first)
                se.wait_ge(unit_done, u.at(1))
                activation(dt_rows[0:64, 0, :], banks[2 * u.r][0:64, 0:T], ACT.Identity, bias=small[0:64, DTB_COL:DTB_COL + 1]).then_inc(evac, 1)
                se.wait_ge(evac, first + 1)
                tally.up(activation(run_rows[0:64, 0, :], dt_rows[0:64, 0, :], ACT.Abs))
                tally.wait(se)
                tally.up(activation(run_rows[0:64, 0, :], run_rows[0:64, 0, :], ACT.Exp, scale=-1.0))
                tally.wait(se)
                activation(run_rows[0:64, 0, :], run_rows[0:64, 0, :], ACT.Ln, bias=ones[0:64, 0:1]).then_inc(dt_soft, 1)
                for i in range(4):
                    store("ssd_in", 1 + i, lambda s: flat(act[:, 4 * i + 2 * s:4 * i + 2 * s + 2, :]), ACT.Silu)
                se.wait_ge(pads, 1)
                for i in range(13):
                    if i < 12:
                        u = Unit(first + 5 + i)
                        se.wait_ge(unit_done, u.at(1))
                        if i >= 1:
                            se.wait_ge(conv_done, i)
                        for s in range(2):
                            ins = activation(conv_buf[:, 2 * s:2 * s + 2, 2:2 + T],
                                             banks[2 * u.r + s][:, :].rearrange("p (j t) -> p j t", t=T), ACT.Copy)
                        ins.then_inc(evac, 1)
                    if i >= 1:
                        se.wait_ge(conv_done, i)
                        t = arena[:, 4 * (i - 1) * T:4 * i * T]
                        activation(t, t, ACT.Silu).then_inc(xs_ready, 1)
                for g in range(8):
                    for d in range(2):
                        se.wait_ge(seg_ready, 2 * g + d + 1)
                        activation(ssd_seg[g % 2][d], ssd_seg[g % 2][d], ACT.Exp).then_inc(decay_exp, 1)
                for half in range(2):
                    se.wait_ge(y_gated, 4 * half + 4)
                    if half == 0:
                        se.wait_ge(pair_ready, 16)
                    activation(flat((sq, hT)[half][:, :, :]), arena[:, 8 * half * T:8 * (half + 1) * T], ACT.Square).then_inc(y_sq, 1)
                se.wait_ge(y_sum, 1)
                activation(std[:, 0:T], bank_sum[:, 0:T], ACT.Sqrt, bias=small[:, 0:1], scale=1.0 / 2048).then_inc(y_std, 1)

            def load_biases():
                for half, low in ((0, -2), (1, -3)):
                    for i in range(6):
                        src = bass.AP(tensor=A["na_rpb_2"].tensor, offset=(low + i + 7) * 31 + 15 - 63,
                                      ap=[[1, 64], [15 * 31, 16], [1, 64]])
                        nc.scalar.dma_start(na_bias[64 * half:64 * half + 64, :, i, :], src).then_inc(rpb_in, 16)

            def na():
                norm("mix_1", meanwhile=load_biases)
                first = base["na_in"]

                def roots(n):
                    se.wait_ge(qk_sum, n + 1)
                    if n >= 1:
                        se.wait_ge(qk_ready, n)
                    for j in range(2):
                        ins = activation(std[:, j * 2 * T:(j + 1) * 2 * T], banks[6 + j][:, :], ACT.Sqrt, bias=small[:, 0:1], scale=1.0 / 64)
                    ins.then_inc(qk_std, 1)
                for c in range(4):
                    u = Unit(first + c)
                    dst = (na_q, na_k)[c // 2]
                    se.wait_ge(unit_done, u.at(1))
                    if c >= 2:
                        se.wait_ge(qk_sum, c - 1)
                    for s in range(2):
                        activation(flat(sq[:, 4 * (c % 2) + 2 * s:4 * (c % 2) + 2 * s + 2, :]), banks[2 * u.r + s][:, :], ACT.Square)\
                            .then_inc(qk_raw, 1)
                    nc.scalar.activation(flat(dst[:, 4 * (c % 2):4 * (c % 2) + 2, :]), banks[2 * u.r][:, :], ACT.Copy).then_inc(qk_sq, 1)
                    activation(flat(dst[:, 4 * (c % 2) + 2:4 * (c % 2) + 4, :]), banks[2 * u.r + 1][:, :], ACT.Copy).then_inc(evac, 1)
                    if c >= 1:
                        roots(c - 1)
                store_tokens("na_in", 4, na_v)
                roots(3)
                store_tokens("na_in", 5, na_v, 512)
                attention(NA)

            def ple(stage):
                i = int(stage[4])
                se.wait_ge(evac, base[stage])
                nc.scalar.dma_start(p_tok, A["p_2"][i, 0].rearrange("(a p) m -> p a m", p=P)).then_inc(p_in, 16)
                norm(stage)
                for c in range(2):
                    store(stage, c, lambda s: flat(act[:, 4 * c + 2 * s:4 * c + 2 * s + 2, :]), ACT.Sigmoid)
                se.wait_ge(p_tr, i + 1)
                activation(flat(pT), bank_x[:, :], ACT.Copy).then_inc(p_cp, 1)
                for c in range(2):
                    store(stage, 2 + c, lambda s: flat(act[:, 8 + 4 * c + 2 * s:8 + 4 * c + 2 * s + 2, :]))
                se.wait_ge(evac, base[stage] + 4)
                activation(sq[:, :, :], act[:, 8:16, :], ACT.Square).then_inc(post_sq, 1)
                se.wait_ge(post_sum, i + 1)
                activation(std[:, 0:T], bank_sum[:, 0:T], ACT.Sqrt, bias=small[:, 0:1], scale=1.0 / D).then_inc(post_std, 1)

            for stage in stages:
                if stage == "even_in":
                    even_mixer()
                if stage == "s5_prep":
                    s5_prep()
                if stage == "s5_tab":
                    s5_tables()
                if stage == "s5_in":
                    s5_in()
                if stage == "s5_glu":
                    s5_glu()
                if stage == "moe":
                    moe()
                if stage == "ssd_in":
                    ssd()
                if stage == "na_in":
                    na()
                if stage == "even_ffn":
                    even_ffn()
                if stage[:5] in ("ffn1_", "ffn2_"):
                    ffn(stage, stage)
                if stage == "final":
                    norm("final")
                if stage[:4] == "ple_":
                    ple(stage)

        @block.vector
        def _(ve):
            tally = Tally(v_chain)

            def input_in():
                for b in range(4):
                    ve.wait_ge(x_tr, b + 1)
                    i = nc.vector.tensor_copy(xT[:, 2 * b:2 * b + 2, :], banks[b][:, :].rearrange("p (k t) -> p k t", t=T))
                i.then_inc(x_ready, 1)

            def vectors_in():
                ve.wait_ge(vec_tr, 1)
                for t in range(5):
                    n = VEC_ROWS[t]
                    i = nc.vector.tensor_copy(vc[:, t, 0:n], (bank_x if t < 4 else bank_sum)[:, (t % 4) * P:(t % 4) * P + n])
                i.then_inc(vec_ready, 1)
                ve.wait_ge(vec_ready, 1)

            silus = [0]

            def norm(name):
                n, gain, shift = NORMS[name]
                ve.wait_ge(std_ready, n + 1)
                tally.up(nc.vector.reciprocal(rs[:, 0:T], std[:, 0:T]))
                tally.wait(ve)
                for k in range(KD):
                    ins = nc.vector.scalar_tensor_tensor(
                        out=(xT if name == "final" else hT)[:, k, :], in0=xT[:, k, :], scalar=gain(k), in1=rs[:, 0:T],
                        op0=ALU.mult, op1=ALU.mult)
                    if name != "final":
                        ins.then_inc(scaled if shift else h_ready, 1)
                if name == "final":
                    ins.then_inc(x_ready, 1)

            def mod_products(u, parts, before):
                for s in range(2):
                    ve.wait_ge(slot_full[2 * u.r + s], u.full())
                for k in range(KD):
                    for s in range(2):
                        w, c = slot(u, s, KD)[:, k, :], csil[:, k:k + 1]
                        if k == 0:
                            ins = nc.vector.tensor_scalar(parts[:, s, :], w, c, None, ALU.mult)
                        else:
                            ve.wait_ge(mod_dve, before + (2 * (k - 1) + s + 1))
                            ins = nc.vector.scalar_tensor_tensor(out=parts[:, s, :], in0=w, scalar=c, in1=parts[:, s, :],
                                                                 op0=ALU.mult, op1=ALU.add)
                        ins.then_inc(mod_dve, 1)

            def mod_out(u, m, i, bank):
                ve.wait_ge(unit_done, u.at(1))
                col = i * 4
                dst, bias = ((mods[:, m, col:col + 4], vc[:, 2, 24 * m + col:24 * m + col + 4]) if isinstance(i, int) else
                             (mods[:, m, bass.ds(col, 4)], vc[:, 2, bass.ds(col + 24 * m, 4)]))
                nc.vector.tensor_tensor(dst, bank[:, 0:4], bias, ALU.add).then_inc(evac, 1)

            def mod_gain(m, last):
                name = ("e_norm_mix", "e_norm_ffn", "o_norm_mix", "o_norm_ffn")[m]
                ve.wait_ge(evac, last + 1)
                nc.vector.scalar_tensor_tensor(out=gains[:, m, :], in0=mods[:, m, KD:2 * KD], scalar=1.0,
                                               in1=vcol(name, 0, KD), op0=ALU.add, op1=ALU.mult).then_inc(mod_ready, 1)

            def mod_em():
                ve.wait_ge(csil_ready, 1)
                for i in range(7):
                    if i < 6:
                        mod_products(Unit(base["mod_em"] + i), em_parts(i), MOD_STEPS * i)
                    if i == 0:
                        input_in()
                    if i == 1:
                        vectors_in()
                    if i >= 1:
                        u = Unit(base["mod_em"] + i - 1)
                        mod_out(u, 0, i - 1, banks[2 * u.r])
                mod_gain(0, base["mod_em"] + 5)

            def even_ffn():
                norm("ef")
                first = base["even_ffn"]

                def gate_up(u, i):
                    ve.wait_ge(silu_ready, i + (silus[0] + 1))
                    gate_times_up(u, i)

                def products(u, which, i, place):
                    ve.wait_ge(unit_done, u.at(1 - 2 * SETS))
                    mod_products(u, ffn_mod_parts(place), (i + (6 * which + 6)) * MOD_STEPS)

                def modulation(u, which, i, place):
                    mod_out(u, 2 + which, i, banks[2 * u.r])

                def down(u, i):
                    ve.wait_ge(unit_done, u.at(1))
                    add_to_x(u, i, lambda k: mods[:, 1, 16 + k:17 + k])
                mod_in_ffn(ve, first, gate_up, modulation, down, early=products)
                silus[0] += GU_UNITS
                mod_gain(2, base["even_ffn"] + STAGE_UNITS["even_ffn"] - 1)
                mod_gain(3, base["even_ffn"] + STAGE_UNITS["even_ffn"] - 1)

            def add_to_x(u, i, gate):
                x = xT[:, 2 * i:2 * i + 2, :].rearrange("p k t -> p (k t)")
                if not callable(gate):
                    nc.vector.scalar_tensor_tensor(out=x, in0=banks[u.r * 2][:, :], scalar=gate, in1=x,
                                                   op0=ALU.mult, op1=ALU.add).then_inc(evac, 1)
                    return
                for t in range(2):
                    xt = xT[:, 2 * i + t, :]
                    ins = nc.vector.scalar_tensor_tensor(out=xt, in0=banks[u.r * 2][:, t * T:(t + 1) * T],
                                                         scalar=gate(2 * i + t), in1=xt, op0=ALU.mult, op1=ALU.add)
                ins.then_inc(evac, 1)

            def gate_times_up(u, i):
                nc.vector.tensor_tensor(act[:, bass.ds(i * 2, 2), :].rearrange("p k t -> p (k t)"), silu_g[:, u.r, :],
                                        banks[2 * u.r + 1][:, :], ALU.mult).then_inc(evac, 1)

            def low_part(u, s, kk, high, before):
                ve.wait_ge(w_high, before + (s + 1))
                nc.vector.tensor_tensor(slot(u, s, kk, rounded=True), slot(u, s, kk), as_f(high), ALU.subtract).then_inc(w_low, 1)

            def ffn(stage, name, gate):
                first, n = base[stage], SPLIT.index(stage)

                def gate_up(u, i):
                    for s in range(2):
                        low_part(u, s, KD, gate_up_high(stage, u, s), slots_before(stage, i))

                def down(i):
                    for s in range(2):
                        low_part(Unit(first + GU_UNITS + i), s, 11, down_high(i, s), slots_before(stage, GU_UNITS + i))

                def hidden(i):
                    ve.wait_ge(act_high, i + (GU_UNITS * n + 1))
                    pair = act[:, 2 * i:2 * i + 2, :] if isinstance(i, int) else act[:, bass.ds(i * 2, 2), :]
                    high = act_hi[:, 2 * i:2 * i + 2, :] if isinstance(i, int) else act_hi[:, bass.ds(i * 2, 2), :]
                    low = act_lo[:, 2 * i:2 * i + 2, :] if isinstance(i, int) else act_lo[:, bass.ds(i * 2, 2), :]
                    nc.vector.tensor_tensor(low, pair, as_f(high), ALU.subtract).then_inc(act_low, 1)

                def step(u, i):
                    if u.c == first + GU_UNITS - 1:
                        down(0)
                    else:
                        gate_up(next_unit(u), i + 1)
                    ve.wait_ge(silu_ready, i + (silus[0] + 1))
                    gate_times_up(u, i)
                    if u.c > first:
                        hidden(i - 1)

                gate_up(Unit(first), 0)
                norm(name)
                for k in range(KD):
                    ve.wait_ge(h_high, KD * n + k + 1)
                    nc.vector.tensor_tensor(h_lo[:, k, :], hT[:, k, :], as_f(h_hi[:, k, :]), ALU.subtract).then_inc(h_low, 1)
                step(Unit(first), 0)
                repeat(ve, first + 1, GU_UNITS - 1, lambda u, i: step(u, i + 1))
                silus[0] += GU_UNITS
                hidden(GU_UNITS - 1)
                for i in range(DN_UNITS):
                    if i + 1 < DN_UNITS:
                        down(i + 1)
                    u = Unit(first + GU_UNITS + i)
                    ve.wait_ge(unit_done, u.at(1))
                    add_to_x(u, i, gate)

            def like(t, mask):
                return t.rearrange("p (b c) -> p b c", c=64) if len(mask.shape) == 3 else t

            def attention(at):
                def maxima(h):
                    g = at.first + h
                    ve.wait_ge(score_ready, g + 1)
                    if h >= 2:
                        ve.wait_ge(prob_tr, g - 1)
                    for a in range(2):
                        tally.up(nc.vector.tensor_tensor_reduce(
                            out=like(probs[:, h % 2, at.span(a)], at.mask(h, a)), in0=like(banks[h % 2][:, at.span(a)], at.mask(h, a)),
                            in1=at.mask(h, a), scale=1.0,
                            scalar=-3e38, op0=ALU.add, op1=ALU.max, accum_out=row_max[:, h % 2, a:a + 1]))
                    tally.wait(ve)
                    nc.vector.tensor_scalar(row_max[:, h % 2, :], row_max[:, h % 2, :], -1.0, None, ALU.mult).then_inc(score_max, 1)

                def divide(h):
                    ve.wait_ge(prob_exp, at.first + h + 1)
                    tally.up(nc.vector.reciprocal(row_inv[:, h % 2, :], row_sum[:, h % 2, :]))
                    tally.wait(ve)
                    for a in range(2):
                        ins = nc.vector.tensor_scalar(probs[:, h % 2, at.span(a)], probs[:, h % 2, at.span(a)],
                                                      row_inv[:, h % 2, a:a + 1], None, ALU.mult)
                    ins.then_inc(prob_ready, 1)

                for step in range(at.heads + 1):
                    if step < at.heads:
                        maxima(step)
                    if step >= 1:
                        divide(step - 1)
                    if at is FOX and has("mod_ef") and step in EF_AT:
                        i = EF_AT[step]
                        mod_out(Unit(base["mod_ef"] + i), 1, i, ef_bank(i))

            def even_mixer():
                norm("em")
                ve.wait_ge(soft_ready, 1)
                x = gate_in[0:8, 2, :]
                tally.up(nc.vector.tensor_scalar(x, x, 0.0, None, ALU.min))
                tally.wait(ve)
                tally.up(nc.vector.tensor_tensor(x, x, gate_low[0:8, 0, :], ALU.subtract))
                tally.wait(ve)
                tally.up(nc.vector.tensor_tensor_scan(fox_cum[0:8, 0, :], ones[0:8, :], x, 0.0, ALU.mult, ALU.subtract))
                ve.wait_ge(soft_ready, 2)
                x = gate_in[:, 0:2, :]
                tally.up(nc.vector.tensor_scalar(x, x, 0.0, None, ALU.min))
                tally.wait(ve)
                tally.up(nc.vector.tensor_tensor(x, x, soft[:, 0:2, :], ALU.subtract))
                tally.wait(ve)
                for j in range(2):
                    tally.up(nc.vector.tensor_tensor_scan(gla_b[:, j, :], ones[:, :], gate_in[:, j, :], 0.0, ALU.mult, ALU.add))
                tally.wait(ve)
                FLOOR = -60.0 * 16.0
                for j in range(2):
                    b = gla_b[:, j, :].rearrange("p (n t) -> p n t", t=GB)
                    tally.up(nc.vector.tensor_tensor(gla_qd[:, j, :].rearrange("p (n t) -> p n t", t=GB), b,
                                                     b[:, :, GB // 2 - 1:GB // 2].to_broadcast([P, NB, GB]), ALU.subtract))
                tally.wait(ve)
                nc.vector.tensor_scalar(gla_qd[:, :, :], gla_qd[:, :, :], -FLOOR, None, ALU.min).then_inc(query_raw, 1)

                def raw(i):
                    if i >= 3:
                        ve.wait_ge(key_used, i - 2)
                    w = P if i < NB // 2 else T
                    for j in range(2):
                        m = i * GB + GB // 2 - 1
                        ins = nc.vector.tensor_scalar(gla_kd[:, 2 * (i % 3) + j, 0:w], gla_b[:, j, 0:w], gla_b[:, j, m:m + 1],
                                                      FLOOR, ALU.subtract, ALU.max)
                    ins.then_inc(key_raw, 1)

                def key(i):
                    ve.wait_ge(key_exp, i + 1)
                    w = P if i < NB // 2 else T
                    kd = gla_kd[:, 2 * (i % 3):2 * (i % 3) + 2, 0:w]
                    nc.vector.tensor_tensor(kd, kd, gla_k[:, :, 0:w], ALU.mult).then_inc(key_ready, 1)

                for i in range(3):
                    raw(i)
                ve.wait_ge(query_exp, 1)
                nc.vector.scalar_tensor_tensor(out=gla_qd[:, :, :], in0=gla_qd[:, :, :], scalar=DH ** -0.5, in1=gla_q[:, :, :],
                                               op0=ALU.mult, op1=ALU.mult).then_inc(query_ready, 1)
                for i in range(NB):
                    key(i)
                    if i + 3 < NB:
                        raw(i + 3)
                ve.wait_ge(key_used, NB)
                for hd in range(4):
                    nc.vector.tensor_tensor(gla_a[:, hd, :], banks[hd][:, 0:3 * P], upper[:, :, :].rearrange("p a t -> p (a t)"),
                                            ALU.mult).then_inc(gla_masked, 1)
                ve.wait_ge(gla_std, 1)
                tally.up(nc.vector.reciprocal(rs[:, :], std[:, :]))
                tally.wait(ve)
                for j in range(2):
                    tally.up(nc.vector.scalar_tensor_tensor(
                        out=gla_o[:, 2 * j:2 * j + 2, :].rearrange("p k t -> p (k t)"), in0=banks[4 + j][:, :],
                        scalar=vcol("e_gla_norm", 0), in1=rs[:, j * 2 * T:(j + 1) * 2 * T], op0=ALU.mult, op1=ALU.mult))
                tally.wait(ve)
                nc.vector.tensor_tensor(act[:, 4:8, :], gla_o[:, :, :], gla_g[:, :, :], ALU.mult).then_inc(gla_done, 1)
                attention(FOX)

            def s5_prep():
                def op(out, a, b, o):
                    tally.wait(ve)
                    tally.up(nc.vector.tensor_tensor(out, a, b, o))

                def op1(out, a, s1, s2, o1, o2=None):
                    tally.wait(ve)
                    tally.up(nc.vector.tensor_scalar(out, a, s1, s2, o1, o2) if o2 else nc.vector.tensor_scalar(out, a, s1, s2, o1))
                lr, li, dt, ang = prm(0), prm(1), prm(3, 2), prm(5)
                mag, k, tmp = prm(6), prm(4), prm(10)
                ve.wait_ge(s5_dt, 1)
                pair = lambda t: t.rearrange("p (g q) -> p g q", g=2)
                step = dt.rearrange("p (g q) -> p g q", q=1).to_broadcast([NS, 2, 64])
                tally.up(nc.vector.tensor_tensor(pair(ang), pair(li), step, ALU.mult))
                nc.vector.tensor_tensor(pair(prm(7)), pair(lr), step, ALU.mult).then_inc(s5_expo, 1)
                op1(k, ang, 0.5 / math.pi, MAGIC, ALU.mult, ALU.add)
                op1(k, k, MAGIC, None, ALU.subtract)
                for part in (TWO_PI_A, TWO_PI_B):
                    tally.wait(ve)
                    tally.up(nc.vector.scalar_tensor_tensor(out=ang, in0=k, scalar=-part, in1=ang, op0=ALU.mult, op1=ALU.add))
                tally.wait(ve)
                nc.vector.tensor_scalar(ang, ang, PI_IN, -PI_IN, ALU.min, ALU.max).then_inc(s5_red, 1)
                ve.wait_ge(s5_sin, 1)
                ve.wait_ge(s5_mag, 1)
                sn, half, cs = prm(8), prm(9), prm(11)
                op(cs, half, half, ALU.mult)
                op1(cs, cs, -2.0, 1.0, ALU.mult, ALU.add)
                op(cs, cs, mag, ALU.mult)
                op(sn, sn, mag, ALU.mult)
                op1(cs, cs, 1.0, None, ALU.subtract)
                op(tmp, lr, lr, ALU.mult)
                op(k, li, li, ALU.mult)
                op(k, k, tmp, ALU.add)
                tally.wait(ve)
                tally.up(nc.vector.reciprocal(k, k))
                fr, fi = prm(12), prm(13)
                op(fr, cs, lr, ALU.mult)
                op(tmp, sn, li, ALU.mult)
                op(fr, fr, tmp, ALU.add)
                op(fi, sn, lr, ALU.mult)
                op(tmp, cs, li, ALU.mult)
                op(fi, fi, tmp, ALU.subtract)
                op(fr, fr, k, ALU.mult)
                tally.wait(ve)
                nc.vector.tensor_tensor(fi, fi, k, ALU.mult).then_inc(s5_rows, 1)
                ve.wait_ge(s5_tr, 1)
                nc.vector.tensor_copy(s5c[:, :, :], bank_x[:, 0:4 * NS].rearrange("p (n i) -> p n i", i=NS)).then_inc(s5_cols, 1)

            def s5_in():
                norm("om")
                ve.wait_ge(raw_in, 64)
                ve.wait_ge(b_zero, 1)
                gain = [s5c[:, 2 + n, :].rearrange("p (i k) -> p i k", k=1).to_broadcast([P, NS, 16]) for n in range(2)]
                t = [silu_g[:, n, :].rearrange("p (i k) -> p i k", k=16) for n in range(3)]
                for n in range(2):
                    tally.up(nc.vector.tensor_tensor(t[0], b_raw[n], gain[0], ALU.mult))
                    tally.up(nc.vector.tensor_tensor(t[1], b_raw[1 - n], gain[1], ALU.mult))
                    tally.wait(ve)
                    for g in range(2):
                        part = slice(64 * g, 64 * g + 64)
                        ins = nc.vector.tensor_tensor(b_wide[n][part, :, 16 * g:16 * g + 16], t[0][part], t[1][part],
                                                      ALU.add if n else ALU.subtract)
                        if n == 0:
                            tally.up(ins)
                    if n == 0:
                        tally.wait(ve)
                ins.then_inc(b_exp, 1)
                tally.up(nc.vector.tensor_reduce(out=parity[:, 0:2], in_=parity[:, 2:10].rearrange("p (a b) -> p b a", b=2),
                                                 axis=mybir.AxisListType.X, op=ALU.add))
                tally.wait(ve)
                ve.wait_ge(bc_tr, 1)
                for n in range(2):
                    for j in range(2):
                        ins = nc.vector.tensor_scalar(c_wide[n][:, :, j, :], c_raw[n], parity[:, j:j + 1], 1.0 - 2.0 * n,
                                                      ALU.mult, ALU.mult)
                ins.then_inc(c_exp, 1)
                ve.wait_ge(tab_ready, NS // 4)
                for i in range(NS + 3):
                    if i < NS:
                        ve.wait_ge(bu_ready, i + 1)
                        if i >= 2:
                            ve.wait_ge(turned, i - 1)
                        both = banks[i % 3][:, :].rearrange("p (c t) -> p c t", c=2)
                        nc.vector.tensor_tensor(s5_t1[i % 2], both, s5_cos[:, i:i + 1, :].to_broadcast([P, 2, T]), ALU.mult)
                        nc.vector.tensor_tensor(s5_t2[i % 2], both, s5_sin_t[:, i:i + 1, :].to_broadcast([P, 2, T]), ALU.mult)\
                            .then_inc(bu_turned, 1)
                    if 1 <= i <= NS:
                        j = i - 1
                        ve.wait_ge(turned, j + 1)
                        if j >= 2:
                            ve.wait_ge(w_ready, j - 1)
                        for c in range(2):
                            ins = nc.vector.tensor_tensor_scan(s5_z[j % 2][:, c, :], s5c[:, 0, j:j + 1].to_broadcast([P, T]),
                                                               s5_t1[j % 2][:, c, :], 0.0, ALU.mult, ALU.add)
                        ins.then_inc(scanned, 1)
                        ve.wait_ge(scanned, j + 1)
                        if j >= 2:
                            ve.wait_ge(w_used, j - 1)
                        nc.vector.tensor_tensor(s5_u1[j % 2], s5_z[j % 2], s5_cos[:, j:j + 1, :].to_broadcast([P, 2, T]), ALU.mult)\
                            .then_inc(back_c, 1)
                    if i >= 6 and (i - 6) % 4 == 0:
                        m = (i - 6) // 4
                        ve.wait_ge(w_used, 4 * m + 4)
                        nc.vector.scalar_tensor_tensor(out=act[:, 8 + m, :], in0=act[:, m, :], scalar=vcol("o_d_skip", m),
                                                       in1=banks[3 + m % 3][:, 0:T], op0=ALU.mult, op1=ALU.add).then_inc(y_read, 1)

            def s5_glu():
                for i in range(2):
                    ve.wait_ge(glu_sig, i + 1)
                    nc.vector.tensor_tensor(flat2(act[:, 4 * i:4 * i + 4, :]), flat2(act[:, 8 + 4 * i:12 + 4 * i, :]),
                                            arena[:, 4 * i * T:4 * (i + 1) * T], ALU.mult).then_inc(evac, 1)

            def moe():
                norm("of")
                first = base["moe"]
                vec = nc.vector
                ve.wait_ge(logit_ready, 1)
                rt = lambda r, c=slice(0, 8): route[:, r:r + 2, c]
                tally.up(vec.tensor_copy(rt(LOGIT), bank_x[:, 0:16].rearrange("p (a e) -> p a e", a=2)))
                tally.up(vec.memset(route[:, GATE:POS + 2, :], 0.0))
                tally.up(vec.tensor_scalar(ramp1[:, 0, :], ramp[:, :], 1.0, None, ALU.add))
                tally.wait(ve)
                for a in range(2):
                    tally.up(vec.max(route[:, TOP + a, 0:8], route[:, LOGIT + a, 0:8]))
                tally.wait(ve)
                for a in range(2):
                    tally.up(vec.max_index(route_u[:, a, :], route[:, TOP + a, 0:8], route[:, LOGIT + a, 0:8]))
                vec.tensor_tensor(rt(MISC, slice(0, 1)), rt(TOP, slice(1, 2)), rt(TOP, slice(0, 1)), ALU.subtract).then_inc(gap_ready, 1)
                tally.wait(ve)
                tally.up(vec.tensor_copy(rt(TOPI), route_u[:, :, :]))
                ve.wait_ge(gap_exp, 1)
                e1, w0, w1 = (rt(MISC, slice(c, c + 1)) for c in (1, 2, 3))
                tally.up(vec.tensor_scalar(w0, e1, 1.0, None, ALU.add))
                tally.wait(ve)
                tally.up(vec.reciprocal(w0, w0))
                tally.wait(ve)
                tally.up(vec.tensor_tensor(w1, e1, w0, ALU.mult))
                tally.wait(ve)
                for a in range(2):
                    for c in range(2):
                        i_col = route[:, TOPI + a, c:c + 1]
                        for dst, w in ((GATE, route[:, MISC + a, 2 + c:3 + c]), (CHOSEN, 1.0)):
                            tally.up(vec.tensor_scalar(route[:, (MISC + 2) + (dst == GATE), 0:8], ramp[:, 0:8], i_col, w, ALU.is_equal, ALU.mult))
                        tally.wait(ve)
                        for dst in (GATE, CHOSEN):
                            tally.up(vec.tensor_tensor(route[:, dst + a, 0:8], route[:, dst + a, 0:8],
                                                       route[:, (MISC + 2) + (dst == GATE), 0:8], ALU.add))
                        tally.wait(ve)
                vec.tensor_copy(route[:, MISC, 4:5], route[:, MISC, 0:1]).then_inc(mask_ready, 1)
                ve.wait_ge(pos_ready, 1)
                tally.up(vec.tensor_copy(counts[0:1, :], bank_sum[0:1, 16:24]))
                vec.tensor_tensor(rt(POS), bank_sum[:, 0:16].rearrange("p (a e) -> p a e", a=2), rt(CHOSEN), ALU.mult).then_inc(scatter_read, 1)
                ve.wait_ge(scatter_read, 1)
                ve.wait_ge(tok_cp, 4)

                def picks(e):
                    for a in range(2):
                        pos, w = route[:, POS + a, bass.ds(e, 1)], route[:, GATE + a, bass.ds(e, 1)]
                        vec.tensor_scalar(pick[:, a, :], ramp1[:, 0, :], pos, None, ALU.is_equal)
                        ins = vec.tensor_scalar(pick_w[:, a, :], ramp1[:, 0, :], pos, w, ALU.is_equal, ALU.mult)
                    ins.then_inc(pick_ready, 1)
                tally.up(vec.tensor_copy(route[:, MISC, 5:6], route[:, MISC, 0:1]))
                tally.wait(ve)
                vec.tensor_copy(route[:, MISC, 6:7], route[:, MISC, 0:1]).then_inc(routed, 1)
                picks(0)
                for i in range(3):
                    tally.wait(ve)
                    vec.tensor_copy(route[:, MISC, 7:8], route[:, MISC, 0:1]).then_inc(hid_low, 1)
                    if i < 2:
                        tally.up(vec.tensor_copy(route[:, MISC, 8:9], route[:, MISC, 0:1]))

                def gate_up_low_parts(u, i, e):
                    for s in range(2):
                        low_part(u, s, KD, gate_up_high("moe", u, s), slots_before("moe", e * 15 + i))

                def down_low_parts(i, e):
                    for s in range(2):
                        low_part(Unit(first + GU_UNITS + i, e * 5), s, 11, down_high(i, s, "moe"),
                                 slots_before("moe", e * 15 + (GU_UNITS + i)))

                def hidden_low(u, i, e):
                    ve.wait_ge(hid_high, e * GU_UNITS + (i + 1))
                    pair = act_r[:, 2 * i:2 * i + 2, :] if isinstance(i, int) else act_r[:, bass.ds(i * 2, 2), :]
                    vec.tensor_tensor(pair[:, :, LOW], banks[2 * u.r][:, HIDDEN].rearrange("p (k t) -> p k t", k=2),
                                      as_f(pair[:, :, HIGH]), ALU.subtract).then_inc(hid_low, 1)

                def units_128(e):
                    gate_up_low_parts(Unit(first, e * 5), 0, e)
                    for j in range(4):
                        ve.wait_ge(gather_cp, e * 4 + (j + 1))
                        vec.tensor_tensor(xg_r[:, 2 * j:2 * j + 2, LOW],
                                          (bank_sum, bank_x)[j % 2][:, 0:2 * P].rearrange("p (k t) -> p k t", k=2),
                                          as_f(xg_r[:, 2 * j:2 * j + 2, HIGH]), ALU.subtract).then_inc(xg_low, 1)

                    def step(u, i):
                        if isinstance(i, int) and i == GU_UNITS - 1:
                            down_low_parts(0, e)
                        else:
                            gate_up_low_parts(next_unit(u), i + 1, e)
                        ve.wait_ge(silu_ready, e * GU_UNITS + (i + (silus[0] + 1)))
                        vec.tensor_tensor(silu_g[:, u.r, HIDDEN], silu_g[:, u.r, 0:COLS], banks[2 * u.r + 1][:, 0:COLS],
                                          ALU.mult).then_inc(evac, 1)
                        if not isinstance(i, int) or i > 0:
                            hidden_low(Unit(u.c - 1, u.v), i - 1, e)
                    step(Unit(first, e * 5), 0)
                    repeat(ve, first + 1, GU_UNITS - 1, lambda u, i: step(u, i + 1), outer=e * 5)
                    hidden_low(Unit(first + GU_UNITS - 1, e * 5), GU_UNITS - 1, e)
                    picks(e + 1)
                    for i in range(1, DN_UNITS):
                        down_low_parts(i, e)

                def expert(e, n):
                    def body(u, i):
                        ve.wait_ge(silu_ready, e * GU_UNITS + (i + (silus[0] + 1)))
                        vec.tensor_tensor(act[:, bass.ds(i * 2, 2), 0:n], silu_g[:, u.r, 0:2 * n].rearrange("p (k t) -> p k t", k=2),
                                          banks[2 * u.r + 1][:, 0:2 * n].rearrange("p (k t) -> p k t", k=2), ALU.mult).then_inc(evac, 1)
                    if n > P:
                        for counter, count in ((w_low, 2 * (GU_UNITS + DN_UNITS)), (hid_low, GU_UNITS), (xg_low, 4)):
                            ve.sem_inc(counter, count)
                        repeat(ve, first, GU_UNITS, body, outer=e * 5)
                        picks(e + 1)
                    else:
                        units_128(e)
                    for j in range(4):
                        ve.wait_ge(scattered, e * 4 + (j + 1))
                        for t in range(2):
                            m = 2 * j + t
                            ins = vec.scalar_tensor_tensor(out=xT[:, m, :], in0=(bank_sum, bank_x)[j % 2][:, t * T:(t + 1) * T],
                                                           scalar=mods[:, 3, 16 + m:17 + m], in1=xT[:, m, :], op0=ALU.mult, op1=ALU.add)
                        ins.then_inc(scatter_read, 1)
                by_count(ve, expert)
                silus[0] += GU_UNITS * E_EXP

            def ssd():
                norm("mix_0")
                first = base["ssd_in"]
                vec = nc.vector
                ve.wait_ge(dt_soft, 1)
                ve.wait_ge(a_exp, 2)
                dt, run = dt_rows[0:64, 0, :], run_rows[0:64, 0, :]
                tally.up(vec.tensor_scalar(dt, dt, 0.0, None, ALU.max))
                tally.wait(ve)
                tally.up(vec.tensor_tensor(dt, dt, run, ALU.add))
                tally.wait(ve)
                step = std[0:64, 2 * T:3 * T]
                tally.up(vec.tensor_scalar(step, dt, small[0:64, 8:9], -1.0, ALU.mult, ALU.mult))
                tally.wait(ve)
                tally.up(vec.tensor_tensor_scan(run, ones[0:64, :], step, 0.0, ALU.mult, ALU.add))
                tally.wait(ve)
                vec.tensor_tensor(run_rows[32:64, 0, :], step[32:64, :], run_rows[32:64, 0, :], ALU.subtract).then_inc(dt_ready, 1)
                ve.wait_ge(evac, first + 5)
                for side in (0, 2 + T):
                    ins = vec.memset(conv_buf[:, :, side:side + 2], 0.0)
                ins.then_inc(pads, 1)
                for i in range(12):
                    ve.wait_ge(evac, first + 6 + i)
                    for tap in range(5):
                        if tap:
                            tally.wait(ve)
                        for t in range(4):
                            j = 4 * i + t
                            out, src = arena[:, j * T:(j + 1) * T], conv_buf[:, t, tap:tap + T]
                            if tap == 0:
                                ins = vec.tensor_scalar(out, src, conv_col(0, j), vcol("ssd_conv_b_2", j), ALU.mult, ALU.add)
                            else:
                                ins = vec.scalar_tensor_tensor(out=out, in0=src, scalar=conv_col(tap, j), in1=out,
                                                               op0=ALU.mult, op1=ALU.add)
                            if tap < 4:
                                tally.up(ins)
                    ins.then_inc(conv_done, 1)
                ve.wait_ge(dt_tr, 1)
                tally.up(vec.tensor_copy(dt_cols_t, bank_x[:, P:2 * P].rearrange("p (s r) -> p s r", s=2)))
                tally.up(vec.tensor_copy(run_cols, bank_x[:, 0:P].rearrange("p (s r) -> p s r", s=2)))
                vec.tensor_copy(d_cols, bank_x[:, T:T + 16]).then_inc(dt_cols, 1)
                ve.wait_ge(dt_cols, 1)

                def read_pairs(g):
                    for n in range(2):
                        ve.wait_ge(pair_ready, 2 * g + n + 1)
                        k = 2 * g + n
                        x = arena[:, k * T:(k + 1) * T]
                        vec.scalar_tensor_tensor(out=x, in0=x, scalar=d_cols[:, k:k + 1], in1=banks[3 + n][:, 0:T],
                                                 op0=ALU.mult, op1=ALU.add).then_inc(pair_read, 1)

                for g in range(8):
                    ve.wait_ge(xs_tr, g + 1)
                    for d in range(2):
                        for s in range(2):
                            ins = vec.tensor_tensor(
                                ssd_x[g % 2][d][:, s, :].rearrange("p (h f) -> p h f", h=4),
                                bank_x[:, s * T:(s + 1) * T].rearrange("p (h f) -> p h f", h=4),
                                dt_cols_t[:, s, 32 * d + 4 * g:32 * d + 4 * g + 4].rearrange("p (h a) -> p h a", a=1)
                                .to_broadcast([P, 4, 64]), ALU.mult)
                    ins.then_inc(xdt_ready, 1)
                    for d in range(2):
                        ve.wait_ge(cb_ready, 2 * g + d + 1)
                        vec.tensor_tensor(ssd_cb[g % 2][d], bank_sum[:, 0:3 * P],
                                          (upper, lower)[d][:, :, :].rearrange("p a t -> p (a t)"), ALU.mult).then_inc(cb_masked, 1)
                    for d in range(2):
                        for n in range(2):
                            ve.wait_ge(rows_ready, 4 * g + 2 * d + n + 1)
                            for j in range(2):
                                hd = 2 * n + j
                                r = 32 * d + 4 * g + hd
                                seg = ssd_seg[g % 2][d][:, hd * 3 * P:(hd + 1) * 3 * P]
                                row = banks[(0, 1, 2, 5)[2 * d + n]][:, j * T:(j + 1) * T]
                                parts = ((0, seg[:, 0:T], row), (1, seg[:, T:3 * P], row[:, P:T])) if d == 0 else \
                                    ((0, seg[:, 0:P], row[:, 0:P]), (1, seg[:, P:3 * P], row))
                                for s, o, src in parts:
                                    ins = vec.tensor_scalar(o, src, run_cols[:, s, r:r + 1], 0.0, ALU.subtract, ALU.min)
                            ins.then_inc(rows_read, 1)
                        ve.wait_ge(rows_read, 4 * g + 2 * d + 2)
                        vec.tensor_copy(route[:, MISC, 8:9], d_cols[:, 0:1]).then_inc(seg_ready, 1)
                    if g >= 1:
                        read_pairs(g - 1)
                    ve.wait_ge(decay_exp, 2 * g + 1)
                    seg = ssd_seg[g % 2][0].rearrange("p (h t) -> p h t", h=4)
                    cb = ssd_cb[g % 2][0].rearrange("p (a t) -> p a t", a=1).to_broadcast([P, 4, 3 * P])
                    vec.tensor_tensor(seg, seg, cb, ALU.mult).then_inc(weights_f, 1)
                read_pairs(7)
                ve.wait_ge(y_std, 1)
                tally.up(vec.reciprocal(rs[:, 0:T], std[:, 0:T]))
                tally.wait(ve)
                for k in range(16):
                    y = arena[:, k * T:(k + 1) * T]
                    vec.scalar_tensor_tensor(out=y, in0=y, scalar=vcol("ssd_norm_2", k), in1=rs[:, 0:T], op0=ALU.mult,
                                             op1=ALU.mult).then_inc(y_normed, 1)

            def na():
                norm("mix_1")
                tally.up(nc.vector.tensor_scalar(qn_col[:, :], vc[:, 1, QN_ROW:QN_ROW + 1], 64 ** -0.5, None, ALU.mult))
                tally.wait(ve)
                for c in range(4):
                    ve.wait_ge(qk_std, c + 1)
                    tally.up(nc.vector.reciprocal(rs[:, :], std[:, :]))
                    tally.wait(ve)
                    ve.wait_ge(evac, base["na_in"] + c + 1)
                    t = flat2((na_q, na_k)[c // 2][:, 4 * (c % 2):4 * (c % 2) + 4, :])
                    gain = qn_col[:, :] if c < 2 else vc[:, 1, KN_ROW:KN_ROW + 1]
                    nc.vector.scalar_tensor_tensor(out=t, in0=t, scalar=gain, in1=rs[:, :], op0=ALU.mult, op1=ALU.mult).then_inc(qk_ready, 1)
                attention(NA)

            def out_product(stage, gate):
                for i in range(STAGE_UNITS[stage]):
                    u = Unit(base[stage] + i)
                    ve.wait_ge(unit_done, u.at(1))
                    for s in range(2):
                        for t in range(2):
                            m = 4 * i + 2 * s + t
                            ins = nc.vector.scalar_tensor_tensor(
                                out=xT[:, m, :], in0=banks[2 * u.r + s][:, t * T:(t + 1) * T],
                                scalar=gate(m) if callable(gate) else gate, in1=xT[:, m, :], op0=ALU.mult, op1=ALU.add)
                    ins.then_inc(evac, 1)

            def ple(stage):
                i = int(stage[4])
                norm(stage)
                ve.wait_ge(post_std, i + 1)
                tally.up(nc.vector.reciprocal(rs[:, 0:T], std[:, 0:T]))
                tally.wait(ve)
                for k in range(KD):
                    tally.up(nc.vector.scalar_tensor_tensor(out=act[:, 8 + k, :], in0=act[:, 8 + k, :],
                                                            scalar=vcol("ple_post_norm_2", 8 * i + k), in1=rs[:, 0:T],
                                                            op0=ALU.mult, op1=ALU.mult))
                tally.wait(ve)
                tally.up(nc.vector.tensor_tensor(act[:, 8:16, :], act[:, 8:16, :], act[:, 0:8, :], ALU.mult))
                tally.wait(ve)
                nc.vector.tensor_tensor(xT[:, :, :], xT[:, :, :], act[:, 8:16, :], ALU.add).then_inc(x_ready, 1)

            for stage in stages:
                if stage == "mod_em":
                    mod_em()
                if stage == "mod_ef":
                    mod_gain(1, base["mod_ef"] + 5)
                if stage == "even_in":
                    ve.wait_ge(mod_ready, 1)
                    even_mixer()
                if stage == "even_out":
                    out_product(stage, lambda m: mods[:, 0, 16 + m:17 + m])
                if stage == "s5_prep":
                    s5_prep()
                if stage == "s5_in":
                    ve.wait_ge(mod_ready, 3)
                    s5_in()
                if stage == "s5_glu":
                    s5_glu()
                if stage == "s5_out":
                    out_product(stage, lambda m: mods[:, 2, 16 + m:17 + m])
                if stage == "moe":
                    ve.wait_ge(mod_ready, 4)
                    moe()
                if stage == "ssd_in":
                    ssd()
                if stage == "ssd_out":
                    for i in range(4):
                        u = Unit(base[stage] + i)
                        ve.wait_ge(unit_done, u.at(1))
                        add_to_x(u, i, 1.0)
                if stage == "na_in":
                    na()
                if stage == "na_out":
                    out_product(stage, 1.0)
                if stage == "even_ffn":
                    ve.wait_ge(mod_ready, 2)
                    even_ffn()
                if stage[:5] in ("ffn1_", "ffn2_"):
                    ffn(stage, stage, 0.5)
                if stage == "final":
                    norm("final")
                if stage[:4] == "ple_":
                    ple(stage)

            for b in range(4):
                a, half = divmod(b, 2)
                ve.wait_ge(out_tr, b + 1)
                nc.vector.tensor_copy(sq[:, :, :].rearrange("p k t -> p (k t)")[:, a * D + half * 512:a * D + half * 512 + 512],
                                      banks[b][:, :]).then_inc(out_cp, 1)
    ctx.close()


def kernel(**inputs):
    import numpy as np
    import concourse.bacc as bacc
    from concourse.bass_utils import run_bass_kernel_spmd

    nc = bacc.Bacc("TRN2", target_bir_lowering=False, num_devices=1, dynamic_dma_scratch_size=1024)
    arrays, args = {}, {}
    for name, a in inputs.items():
        a = np.ascontiguousarray(a)
        arrays[f"in_{name}"] = a
        args[name] = nc.dram_tensor(f"in_{name}", a.shape, mybir.dt.from_np(a.dtype), kind="ExternalInput").ap()
    out = nc.dram_tensor("out", (1, T, D), F32, kind="ExternalOutput").ap()
    program(nc, args, out)
    return run_bass_kernel_spmd(nc, [arrays], core_ids=[0]).results[0]["out"]
```
